# Optimizing a Trainium2 kernel written in Bass

```python
import jax, jax.numpy as jnp
from jax import lax
import numpy as np

D_MODEL = 1024
BATCH = 1
SEQ = 1024
DEPTH = 1

PLE_DIM = 256
EPS = 1e-6
N_HEADS = 8
QK_NOPE = 64
QK_ROPE = 32
QK_HEAD = QK_NOPE + QK_ROPE
V_HEAD = 64
Q_LORA = 256
KV_LORA = 128
ROPE_THETA = 10000.0
Q_BLOCK = 128
ATTN_WIDTH = N_HEADS * V_HEAD
POOL_WINDOWS = (2, 4, 8, 16)
POOL_GROUPS = 4
POOL_WIDTH = 512
POOL_GROUP_DIM = POOL_WIDTH // POOL_GROUPS
N_EXPERTS = 32
TOP_K = 4
D_EXPERT = 1024
SWIGLU_ALPHA = 1.702
SWIGLU_LIMIT = 7.0
EXPERT_BLOCK = 128
IN_SPLITS = (Q_LORA, Q_LORA + KV_LORA, Q_LORA + KV_LORA + QK_ROPE,
             Q_LORA + KV_LORA + QK_ROPE + POOL_WIDTH)
IN_PROJ_WIDTH = Q_LORA + KV_LORA + QK_ROPE + POOL_WIDTH + 2 * D_MODEL

kernel_name = "hybrid_mla_pool_moe_ple_block"

def rmsnorm(x, g):
    xf = x.astype(jnp.float32)
    y = xf * lax.rsqrt(jnp.mean(xf * xf, axis=-1, keepdims=True) + EPS)
    return (y * g.astype(jnp.float32)).astype(x.dtype)

def rope(x, cos, sin):
    x1, x2 = jnp.split(x.astype(jnp.float32), 2, axis=-1)
    return jnp.concatenate([x1 * cos - x2 * sin, x2 * cos + x1 * sin], axis=-1).astype(x.dtype)

def mla_branch(q_lat, kv_lat, k_rope_in, positions, g_q_lat, w_q_b, g_kv_lat, w_kv_b,
               g_q_head, g_k_nope, g_k_rope):
    B, S, _ = q_lat.shape
    q = (rmsnorm(q_lat, g_q_lat) @ w_q_b).reshape(B, S, N_HEADS, QK_HEAD)
    q = rmsnorm(q, g_q_head)
    kv = (rmsnorm(kv_lat, g_kv_lat) @ w_kv_b).reshape(B, S, N_HEADS, QK_NOPE + V_HEAD)
    k_nope, v = kv[..., :QK_NOPE], kv[..., QK_NOPE:]
    k_nope = rmsnorm(k_nope, g_k_nope)
    k_rope = rmsnorm(k_rope_in, g_k_rope)

    inv_freq = ROPE_THETA ** (-jnp.arange(0, QK_ROPE, 2, dtype=jnp.float32) / QK_ROPE)
    ang = positions.astype(jnp.float32)[..., None] * inv_freq
    cos, sin = jnp.cos(ang), jnp.sin(ang)
    q = jnp.concatenate([q[..., :QK_NOPE], rope(q[..., QK_NOPE:], cos[:, :, None], sin[:, :, None])], axis=-1)
    k_rope = rope(k_rope, cos, sin)
    k = jnp.concatenate([k_nope, jnp.broadcast_to(k_rope[:, :, None, :], (B, S, N_HEADS, QK_ROPE))], axis=-1)

    n_blocks = S // Q_BLOCK
    qb = q.reshape(B, n_blocks, Q_BLOCK, N_HEADS, QK_HEAD).transpose(1, 0, 3, 2, 4)
    kt = k.transpose(0, 2, 1, 3)
    vt = v.transpose(0, 2, 1, 3)
    scale = 1.0 / np.sqrt(QK_HEAD)
    key_idx = jnp.arange(S)

    def attend(args):
        q_blk, blk = args
        s = jnp.einsum('bhqd,bhkd->bhqk', q_blk, kt).astype(jnp.float32) * scale
        q_idx = blk * Q_BLOCK + jnp.arange(Q_BLOCK)
        mask = q_idx[:, None] >= key_idx[None, :]
        s = jnp.where(mask, s, jnp.float32(-1e30))
        pr = jax.nn.softmax(s, axis=-1).astype(vt.dtype)
        return jnp.einsum('bhqk,bhkd->bhqd', pr, vt)

    out = lax.map(attend, (qb, jnp.arange(n_blocks)))
    return out.transpose(1, 0, 3, 2, 4).reshape(B, S, ATTN_WIDTH)

def pool_branch(u, w_pool, pool_scale):
    B, S, _ = u.shape
    uf = u.astype(jnp.float32).reshape(B, S, POOL_GROUPS, POOL_GROUP_DIM)
    c = jnp.concatenate([jnp.zeros((B, 1, POOL_GROUPS, POOL_GROUP_DIM), jnp.float32),
                         jnp.cumsum(uf, axis=1)], axis=1)
    t = jnp.arange(S)
    means = []
    for g, w in enumerate(POOL_WINDOWS):
        lo = jnp.maximum(t + 1 - w, 0)
        window_sum = c[:, 1:, g] - c[:, lo, g]
        count = (t + 1 - lo).astype(jnp.float32)[:, None]
        means.append(window_sum / count)
    pooled = (jnp.stack(means, axis=2) - uf).astype(u.dtype)
    mixed = jnp.einsum('bsgc,gcd->bsgd', pooled, w_pool)
    return mixed.reshape(B, S, POOL_WIDTH) * pool_scale

def moe(h, w_router, b_router, w_gate_up, b_gate_up, w_down, b_down):
    B, S, D = h.shape
    T = B * S
    A = T * TOP_K
    hf = h.reshape(T, D)
    logits = (hf @ w_router).astype(jnp.float32) + b_router.astype(jnp.float32)
    top_val, top_idx = lax.top_k(logits, TOP_K)
    gates = jax.nn.softmax(top_val, axis=-1)

    expert_flat = top_idx.reshape(A)
    token_flat = jnp.repeat(jnp.arange(T, dtype=jnp.int32), TOP_K)
    gate_flat = gates.reshape(A)
    order = jnp.argsort(expert_flat)
    e_sorted = expert_flat[order]
    counts = jax.ops.segment_sum(jnp.ones((A,), jnp.int32), expert_flat, num_segments=N_EXPERTS)
    padded = (counts + EXPERT_BLOCK - 1) // EXPERT_BLOCK * EXPERT_BLOCK
    start = jnp.cumsum(counts) - counts
    pad_end = jnp.cumsum(padded)
    pad_start = pad_end - padded
    dest = pad_start[e_sorted] + jnp.arange(A, dtype=jnp.int32) - start[e_sorted]

    n_blocks = (A + EXPERT_BLOCK - 1) // EXPERT_BLOCK + N_EXPERTS
    M = n_blocks * EXPERT_BLOCK
    tok_buf = jnp.full((M,), T, jnp.int32).at[dest].set(token_flat[order])
    gate_buf = jnp.zeros((M,), jnp.float32).at[dest].set(gate_flat[order])
    block_expert = jnp.minimum(
        jnp.searchsorted(pad_end, jnp.arange(n_blocks, dtype=jnp.int32) * EXPERT_BLOCK, side='right'),
        N_EXPERTS - 1)
    h_pad = jnp.concatenate([hf, jnp.zeros((1, D), hf.dtype)], axis=0)
    x_blocks = h_pad[tok_buf].reshape(n_blocks, EXPERT_BLOCK, D)

    def expert_block(args):
        xb, e = args
        gu = xb @ w_gate_up[e] + b_gate_up[e]
        gate, up = gu[:, :D_EXPERT], gu[:, D_EXPERT:]
        gate = jnp.minimum(gate, SWIGLU_LIMIT)
        up = jnp.clip(up, -SWIGLU_LIMIT, SWIGLU_LIMIT)
        act = (up + 1.0) * gate * jax.nn.sigmoid(SWIGLU_ALPHA * gate)
        return act @ w_down[e] + b_down[e]

    y = lax.map(expert_block, (x_blocks, block_expert)).reshape(M, D)
    y = y * gate_buf[:, None].astype(y.dtype)
    out = jnp.zeros((T + 1, D), y.dtype).at[tok_buf].add(y)[:T]
    return out.reshape(B, S, D)

def setup_inputs(seed: int = 0) -> dict:
    key = jax.random.key(seed)
    ks = jax.random.split(key, 32)

    def dense(k, shape, fan_in):
        return jax.random.normal(k, shape, jnp.float32) * (fan_in ** -0.5)

    def gain(k, shape):
        return 1.0 + 0.05 * jax.random.normal(k, shape, jnp.float32)

    def bias(k, shape):
        return 0.01 * jax.random.normal(k, shape, jnp.float32)

    L = DEPTH
    x = jax.random.normal(ks[0], (BATCH, SEQ, D_MODEL), jnp.float32)
    p = jax.random.normal(ks[1], (DEPTH, BATCH, SEQ, PLE_DIM), jnp.float32)
    offset = jax.random.randint(ks[2], (BATCH, 1), 0, 1024, dtype=jnp.int32)
    positions = offset + jnp.arange(SEQ, dtype=jnp.int32)[None, :]
    return {
        "x": x,
        "p": p,
        "positions": positions,
        "g_mix": gain(ks[3], (L, D_MODEL)),
        "w_in": dense(ks[4], (L, D_MODEL, IN_PROJ_WIDTH), D_MODEL),
        "g_q_lat": gain(ks[5], (L, Q_LORA)),
        "w_q_b": dense(ks[6], (L, Q_LORA, N_HEADS * QK_HEAD), Q_LORA),
        "g_kv_lat": gain(ks[7], (L, KV_LORA)),
        "w_kv_b": dense(ks[8], (L, KV_LORA, N_HEADS * (QK_NOPE + V_HEAD)), KV_LORA),
        "g_q_head": gain(ks[9], (L, QK_HEAD)),
        "g_k_nope": gain(ks[10], (L, QK_NOPE)),
        "g_k_rope": gain(ks[11], (L, QK_ROPE)),
        "w_pool": dense(ks[12], (L, POOL_GROUPS, POOL_GROUP_DIM, POOL_GROUP_DIM), POOL_GROUP_DIM),
        "pool_scale": gain(ks[13], (L, POOL_WIDTH)),
        "w_attn_out": dense(ks[14], (L, ATTN_WIDTH, D_MODEL), ATTN_WIDTH),
        "w_pool_out": dense(ks[15], (L, POOL_WIDTH, D_MODEL), POOL_WIDTH),
        "w_o": dense(ks[16], (L, D_MODEL, D_MODEL), D_MODEL),
        "g_ffn": gain(ks[17], (L, D_MODEL)),
        "w_router": dense(ks[18], (L, D_MODEL, N_EXPERTS), D_MODEL),
        "b_router": bias(ks[19], (L, N_EXPERTS)),
        "w_gate_up": dense(ks[20], (L, N_EXPERTS, D_MODEL, 2 * D_EXPERT), D_MODEL),
        "b_gate_up": bias(ks[21], (L, N_EXPERTS, 2 * D_EXPERT)),
        "w_down": dense(ks[22], (L, N_EXPERTS, D_EXPERT, D_MODEL), D_EXPERT),
        "b_down": bias(ks[23], (L, N_EXPERTS, D_MODEL)),
        "g_ple": gain(ks[24], (L, D_MODEL)),
        "w_ple_gate": dense(ks[25], (L, D_MODEL, D_MODEL), D_MODEL),
        "w_ple": dense(ks[26], (L, PLE_DIM, D_MODEL), PLE_DIM),
    }

def reference(x, p, positions, g_mix, w_in, g_q_lat, w_q_b, g_kv_lat, w_kv_b, g_q_head,
              g_k_nope, g_k_rope, w_pool, pool_scale, w_attn_out, w_pool_out, w_o, g_ffn,
              w_router, b_router, w_gate_up, b_gate_up, w_down, b_down, g_ple, w_ple_gate, w_ple):
    for i in range(DEPTH):
        h = rmsnorm(x, g_mix[i])
        proj = h @ w_in[i]
        q_lat, kv_lat, k_rope_in, pool_in, gate_logits = jnp.split(proj, IN_SPLITS, axis=-1)
        y_attn = mla_branch(q_lat, kv_lat, k_rope_in, positions, g_q_lat[i], w_q_b[i],
                            g_kv_lat[i], w_kv_b[i], g_q_head[i], g_k_nope[i], g_k_rope[i]) @ w_attn_out[i]
        y_pool = pool_branch(pool_in, w_pool[i], pool_scale[i]) @ w_pool_out[i]
        gate_a, gate_p = jnp.split(jax.nn.sigmoid(gate_logits), 2, axis=-1)
        x = x + (gate_a * y_attn + gate_p * y_pool) @ w_o[i]
        x = x + moe(rmsnorm(x, g_ffn[i]), w_router[i], b_router[i], w_gate_up[i], b_gate_up[i],
                    w_down[i], b_down[i])
        ple_gate = jax.nn.sigmoid(rmsnorm(x, g_ple[i]) @ w_ple_gate[i])
        x = x + ple_gate * (p[i] @ w_ple[i])
    return x


_drawn_inputs = setup_inputs


def setup_inputs(seed=0):
    import zlib

    import numpy as np

    out = dict(_drawn_inputs(seed))
    spreads = {}
    factors = {'g_q_lat': 3.883,
     'g_kv_lat': 3.194,
     'g_q_head': 3.957,
     'g_k_nope': 3.921,
     'g_k_rope': 6.605,
     'b_gate_up': 8.0,
     'b_down': 8.0,
     'g_ple': 25.175,
     'b_router': 2.787}
    for name, (base, spread) in spreads.items():
        noise = np.random.default_rng([zlib.crc32(name.encode()), seed]).standard_normal(out[name].shape)
        drawn = base * np.exp(spread * noise) if base else spread * noise
        out[name] = __import__('jax').numpy.asarray(drawn.astype(out[name].dtype))
    for name, factor in factors.items():
        out[name] = (out[name] * factor).astype(out[name].dtype)
    return out
```

```python
from contextlib import ExitStack

import numpy as np

import concourse.bass as bass
from concourse import mybir

ALU = mybir.AluOpType
ACT = mybir.ActivationFunctionType
AX = mybir.AxisListType
F32 = mybir.dt.float32
BF16 = mybir.dt.bfloat16
I32 = mybir.dt.int32
U32 = mybir.dt.uint32

P = 128
EPS = 1e-6
ROPE_THETA = 10000.0
SWIGLU_ALPHA = 1.702
SWIGLU_LIMIT = 7.0
TOP_K = 4
POOL_WINDOWS = (2, 4, 8, 16)
NEG = -1e30
BANK = 512

WIDTHS = (128, 144, 160, 192)
WIDTH = WIDTHS[-1]
ITEM_ROWS = 64
ITEM_FIELDS = 5


def two_stage_loop(eng, tiles, lead, follow):
    lead(0, 0)
    with eng.Fori(0, tiles // 2 - 1) as i:
        for b in (0, 1):
            lead(2 * i + (b + 1), 1 - b)
            follow(2 * i + b, b)
    lead(tiles - 1, 1)
    follow(tiles - 2, 0)
    follow(tiles - 1, 1)


def pair_loop(eng, tiles, body, first=0):
    with eng.Fori(first // 2, tiles // 2) as i:
        for b in (0, 1):
            body(2 * i + b, b)


def view(arena, start, *dims):
    flat = arena[:, start:start + int(np.prod(dims))]
    if len(dims) == 1:
        return flat
    names = "abc"[:len(dims)]
    return flat.rearrange(
        f"p ({' '.join(names)}) -> p {' '.join(names)}", **{n: d for n, d in zip(names, dims)})


def build(nc, x, p, positions, g_mix, w_in, g_q_lat, w_q_b, g_kv_lat, w_kv_b, g_q_head, g_k_nope,
          g_k_rope, w_pool, pool_scale, w_attn_out, w_pool_out, w_o, g_ffn, w_router, b_router,
          w_gate_up, b_gate_up, w_down, b_down, g_ple, w_ple_gate, w_ple, out):
    S, D = x.shape[1:]
    T = S // P
    K = D // P
    QL, KL = g_q_lat.shape[1], g_kv_lat.shape[1]
    HD = g_q_head.shape[1]
    NOPE, ROPE = g_k_nope.shape[1], g_k_rope.shape[1]
    HALF = ROPE // 2
    H = w_q_b.shape[2] // HD
    V = w_kv_b.shape[2] // H - NOPE
    LAT = QL + KL + ROPE
    G, C = w_pool.shape[1:3]
    POOL = G * C
    GATE_A = LAT + POOL
    GATE_P = GATE_A + D
    E = w_router.shape[2]
    FF = w_down.shape[2]
    KF = FF // P
    PLE = p.shape[3]
    KP = PLE // P
    AW = H * V
    KA, KO = AW // P, POOL // P
    HP = H // 2
    SLOTS = E * S
    ROWS = S * TOP_K

    x2d, out2d = x[0], out[0]
    w_in, w_q_b, w_kv_b, w_attn_out, w_pool_out, w_o = (
        a[0] for a in (w_in, w_q_b, w_kv_b, w_attn_out, w_pool_out, w_o))
    w_gate_up, w_down, w_ple_gate, w_ple, p2d = w_gate_up[0], w_down[0], w_ple_gate[0], w_ple[0], p[0, 0]

    x1_dram = nc.dram_tensor("x1_rows", [S, D], F32).ap()
    h2_dram = nc.dram_tensor("h2_rows", [S, D], F32).ap()
    list_dram = nc.dram_tensor("slot_tokens", [SLOTS, 1], I32).ap()
    y_dram = nc.dram_tensor("expert_rows", [S * TOP_K + WIDTH, D], F32).ap()
    item_dram = nc.dram_tensor("items", [ITEM_ROWS, ITEM_FIELDS], I32).ap()

    with ExitStack() as top:
        def sb(name, shape, dt=F32, ctx=top):
            return ctx.enter_context(nc.sbuf_tensor(name, shape, dt))

        arena_w = sb("arena_w", [P, 3 * 8192])
        arena_h = sb("arena_h", [P, 8192])
        arena_m = sb("arena_m", [P, 8192])
        arena_a = sb("arena_a", [P, 8192])
        ident = sb("ident", [P, P])
        gain_row = sb("gain_row", [P, D])
        eps = sb("eps", [P, 1])
        iota_e = sb("iota_e", [P, E])
        dest_all = sb("dest_all", [P, T, TOP_K], I32)
        gates_all = sb("gates_all", [P, T, TOP_K])
        items = sb("items_row", [1, ITEM_ROWS * ITEM_FIELDS], I32)
        bias_gu = sb("bias_gu", [P, E * 2 * KF])
        bias_dn = sb("bias_dn", [P, E * K])
        banks = [top.enter_context(nc.psum_tensor(f"bank{i}", [P, BANK], F32)) for i in range(8)]

        always = top.enter_context(nc.semaphore("always"))

        def wait_value(eng, sem, value):
            if not isinstance(value, int):
                value = eng.to_reg(value)
                eng.wait_ge(always, 1)
            eng.wait_ge(sem, value)

        hT = view(arena_h, 0, K, S)
        mT = view(arena_m, 0, K, S)
        attnT = view(arena_a, 0, KA, S)
        mixedT = view(arena_a, KA * S, KO, S)
        q_full = view(arena_w, 0, T, H, HD)
        k_full = view(arena_w, T * H * HD, T, H, HD)
        v_full = view(arena_w, 2 * T * H * HD, T, H, V)
        spare_w = 2 * T * H * HD + T * H * V

        def stage(name):
            ctx = ExitStack()
            sems = {}

            def sem(n):
                if n not in sems:
                    sems[n] = ctx.enter_context(nc.semaphore(f"{name}_{n}"))
                return sems[n]
            return ctx, sem

        def front():
            ctx, sem = stage("front")
            with ctx:
                xt = [view(arena_a, D * (5 + b), D) for b in (0, 1)]
                junk = view(arena_a, 0, D)
                xn = [view(arena_a, D * (1 + b), D) for b in (0, 1)]
                hts = [view(arena_a, D * (3 + b), K, P) for b in (0, 1)]
                latn = [view(arena_m, 400 * b, QL + KL) for b in (0, 1)]
                krn = [view(arena_m, 800 + 32 * b, ROPE) for b in (0, 1)]
                latT = [view(arena_m, 1024 + 512 * b, 3, P) for b in (0, 1)]
                q_tmp = [view(arena_m, 2048 + 768 * b, H, HD) for b in (0, 1)]
                k_tmp = [view(arena_m, 3584 + 512 * b, H, NOPE) for b in (0, 1)]
                sq_q = view(arena_m, 4608, H, HD)
                sq_k = view(arena_m, 5376, H, NOPE)
                qr = view(arena_m, 5888, H, ROPE)
                ra = view(arena_m, 6144, H, ROPE)
                rb = view(arena_m, 6400, H, ROPE)
                kra = view(arena_m, 6656, ROPE)
                krb = view(arena_m, 6688, ROPE)
                krr = view(arena_m, 6720, ROPE)
                g_lat3 = view(arena_m, 6752, 3)
                g_qh = view(arena_m, 6760, HD)
                g_kn = view(arena_m, 6856, NOPE)
                g_kr = view(arena_m, 6920, ROPE)
                stat = view(arena_m, 6960, 128)
                ms = [stat[:, b:b + 1] for b in (0, 1)]
                rms = [stat[:, 2 + b:3 + b] for b in (0, 1)]
                rstd = [stat[:, 4 + b:5 + b] for b in (0, 1)]
                ms3, rms3, rs3 = stat[:, 8:11], stat[:, 12:15], stat[:, 16:19]
                msh, rmsh, rsh = stat[:, 20:36], stat[:, 40:56], stat[:, 60:76]
                cc = view(arena_m, 7168, T, ROPE)
                sn = view(arena_m, 7168 + T * ROPE, T, ROPE)
                pos_i = stat.bitcast(I32)[:, 80:88]
                pos_f = stat[:, 90:98]
                inv = stat[:, 100:116]
                ang, turns, red = (view(arena_m, 2048 + 128 * j, T, HALF) for j in range(3))
                ang_c, turns_c = (view(arena_m, 2048 + 128 * j, T, HALF) for j in (3, 4))

                w_lat = view(arena_w, spare_w, K, LAT)
                w_q = view(arena_w, spare_w + K * LAT, 2, H * HD)
                w_kv = view(arena_w, spare_w + K * LAT + 2 * H * HD, H * (NOPE + V))
                b_rows = view(arena_h, 0, 6, P)

                TP0, TP1, BL, BT, Q0, Q1, KV0, KV1 = banks
                n_bias = (E * 2 * KF + E * K) // P

                with nc.Block() as block:
                    @block.sync
                    def _(sp):
                        sp.dma_start(xt[0], x2d[0:P, :]).then_inc(sem("x0"), 16)
                        sp.dma_start(xt[1], x2d[P:2 * P, :]).then_inc(sem("x1"), 16)
                        sp.dma_start(gain_row[:, :], g_mix[0].partition_broadcast(P)).then_inc(sem("gain"), 16)
                        sp.dma_start(w_lat, w_in[:, 0:LAT].rearrange("(k p) n -> p k n", p=P)).then_inc(sem("w_lat"), 16)
                        sp.dma_start(w_q, w_q_b.rearrange("(k p) n -> p k n", p=P)).then_inc(sem("w_q"), 16)
                        sp.dma_start(w_kv, w_kv_b).then_inc(sem("w_kv"), 16)
                        with sp.Fori(1, T // 2) as i:
                            for b in (0, 1):
                                wait_value(sp, sem("xn_ready"), 2 * i + (b - 1))
                                sp.dma_start(xt[b], x2d[bass.ds(i * (2 * P) + b * P, P), :]).then_inc(sem(f"x{b}"), 16)

                    @block.gpsimd
                    def _(pool):
                        pool.memset(eps[:, :], EPS).then_inc(always, 1)
                        pool.memset(ident[:, :], 0.0).then_inc(sem("pc"), 1)
                        pool.iota(iota_e[:, :], pattern=[[1, E]], base=0, channel_multiplier=0,
                                  allow_small_or_imprecise_dtypes=True).then_inc(sem("pc"), 1)
                        for j in range(HALF):
                            f = float(np.float32(ROPE_THETA) ** np.float32(-2 * j / ROPE))
                            pool.memset(inv[:, j:j + 1], f).then_inc(sem("pc"), 1)
                        pool.wait_ge(sem("pc"), 1)
                        pool.affine_select(out=ident[:, :], in_=ident[:, :], compare_op=ALU.not_equal, fill=1.0,
                                           base=0, pattern=[[-1, P]], channel_multiplier=1).then_inc(sem("ident"), 1)
                        pool.dma_start(pos_i, positions[0].rearrange("(t p) -> p t", p=P), allow_slow_non_contiguous=True).then_inc(sem("pos"), 16)
                        pool.dma_start(g_lat3[:, 0:2], g_q_lat[0].rearrange("(k p) -> p k", p=P), allow_slow_non_contiguous=True).then_inc(sem("g_small"), 16)
                        pool.dma_start(g_lat3[:, 2:3], g_kv_lat[0].rearrange("(k p) -> p k", p=P), allow_slow_non_contiguous=True).then_inc(sem("g_small"), 16)
                        pool.dma_start(g_qh, g_q_head[0].partition_broadcast(P)).then_inc(sem("g_small"), 16)
                        pool.dma_start(g_kn, g_k_nope[0].partition_broadcast(P)).then_inc(sem("g_small"), 16)
                        pool.dma_start(g_kr, g_k_rope[0].partition_broadcast(P)).then_inc(sem("g_small"), 16)
                        pool.dma_start(b_rows[:, 0:4, :], b_gate_up[0].rearrange("e (f c) -> (e f) c", c=P)
                                       .rearrange("(j r) c -> r j c", r=P)).then_inc(sem("biases"), 16)
                        pool.dma_start(b_rows[:, 4:6, :], b_down[0].rearrange("e (f c) -> (e f) c", c=P)
                                       .rearrange("(j r) c -> r j c", r=P)).then_inc(sem("biases"), 16)
                        pool.wait_ge(sem("g_small"), 80)
                        pool.wait_ge(sem("angles"), 4)

                        def keep_hT(n, b):
                            if isinstance(n, int) and n == 0:
                                pool.wait_ge(sem("bias_psum"), 1)
                            wait_value(pool, sem("hts_ready"), 2 * n + 2)
                            pool.tensor_copy(hT[:, :, bass.ds(n * P, P)], hts[b]).then_inc(sem("hts_kept"), 1)

                        def rotate(n, b):
                            wait_value(pool, sem("q_tmp"), n + 1)
                            gq = g_qh.unsqueeze(1)
                            pool.tensor_tensor(q_full[:, bass.ds(n, 1), :, 0:NOPE].rearrange("p o h d -> p (o h) d"),
                                               q_tmp[b][:, :, 0:NOPE],
                                               gq[:, :, 0:NOPE].broadcast_to([P, H, NOPE]), ALU.mult).then_inc(sem("pq"), 1)
                            pool.tensor_tensor(qr, q_tmp[b][:, :, NOPE:HD],
                                               gq[:, :, NOPE:HD].broadcast_to([P, H, ROPE]), ALU.mult).then_inc(sem("pr"), 1)
                            c_n = cc[:, bass.ds(n, 1), :].broadcast_to([P, H, ROPE])
                            s_n = sn[:, bass.ds(n, 1), :].broadcast_to([P, H, ROPE])
                            wait_value(pool, sem("pr"), 4 * n + 1)
                            pool.tensor_tensor(ra, qr, c_n, ALU.mult).then_inc(sem("pr"), 1)
                            pool.tensor_tensor(rb[:, :, 0:HALF], qr[:, :, HALF:ROPE], s_n[:, :, 0:HALF], ALU.mult).then_inc(sem("pr"), 1)
                            pool.tensor_tensor(rb[:, :, HALF:ROPE], qr[:, :, 0:HALF], s_n[:, :, HALF:ROPE], ALU.mult).then_inc(sem("pr"), 1)
                            wait_value(pool, sem("pr"), 4 * n + 4)
                            pool.tensor_tensor(q_full[:, bass.ds(n, 1), :, NOPE:HD].rearrange("p o h d -> p (o h) d"),
                                               ra, rb, ALU.add).then_inc(sem("pq"), 1)
                            wait_value(pool, sem("k_tmp"), n + 1)
                            pool.tensor_tensor(k_full[:, bass.ds(n, 1), :, 0:NOPE].rearrange("p o h d -> p (o h) d"),
                                               k_tmp[b], g_kn.unsqueeze(1).broadcast_to([P, H, NOPE]), ALU.mult).then_inc(sem("pk"), 1)
                            c_1 = cc[:, bass.ds(n, 1), :].rearrange("p o r -> p (o r)")
                            s_1 = sn[:, bass.ds(n, 1), :].rearrange("p o r -> p (o r)")
                            pool.tensor_tensor(kra, krn[b], c_1, ALU.mult).then_inc(sem("pk"), 1)
                            pool.tensor_tensor(krb[:, 0:HALF], krn[b][:, HALF:ROPE], s_1[:, 0:HALF], ALU.mult).then_inc(sem("pk"), 1)
                            pool.tensor_tensor(krb[:, HALF:ROPE], krn[b][:, 0:HALF], s_1[:, HALF:ROPE], ALU.mult).then_inc(sem("pk"), 1)
                            wait_value(pool, sem("pk"), 5 * n + 4)
                            pool.tensor_tensor(krr, kra, krb, ALU.add).then_inc(sem("pk"), 1)
                            wait_value(pool, sem("pk"), 5 * n + 5)
                            pool.tensor_copy(k_full[:, bass.ds(n, 1), :, NOPE:HD].rearrange("p o h d -> p (o h) d"),
                                             krr.unsqueeze(1).broadcast_to([P, H, ROPE])).then_inc(sem("rotated"), 1)

                        two_stage_loop(pool, T, keep_hT, rotate)

                    @block.tensor
                    def _(pe):
                        pe.wait_ge(sem("ident"), 1)
                        pe.wait_ge(sem("biases"), 32)
                        for j in range(n_bias):
                            t = pe.transpose(banks[4 + j // 4][:, (j % 4) * P:(j % 4 + 1) * P], b_rows[:, j, :], ident[:, :])
                        t.then_inc(sem("bias_psum"), 1)

                        def latents(n, b):
                            wait_value(pe, sem("xn_ready"), n + 1)
                            for k in range(K):
                                t = pe.transpose((TP0, TP1)[k // 4][:, (k % 4) * P:(k % 4 + 1) * P],
                                                 xn[b][:, k * P:(k + 1) * P], ident[:, :])
                            t.then_inc(sem("xT_psum"), 1)
                            wait_value(pe, sem("hts_ready"), 2 * n + 2)
                            if isinstance(n, int) and n == 0:
                                pe.wait_ge(sem("w_lat"), 16)
                            else:
                                wait_value(pe, sem("latn"), n)
                            for k in range(K):
                                m = pe.matmul(BL[:, 0:LAT], hts[b][:, k, :], w_lat[:, k, :], start=(k == 0), stop=(k == K - 1))
                            m.then_inc(sem("lat_psum"), 1)
                            if isinstance(n, int) and n == 0:
                                pe.wait_ge(sem("w_q"), 16)
                                pe.wait_ge(sem("w_kv"), 16)
                                pe.wait_ge(sem("bias_read"), 2)

                        def heads(n, b):
                            wait_value(pe, sem("latn"), n + 1)
                            for j in range(3):
                                t = pe.transpose(BT[:, j * P:(j + 1) * P], latn[b][:, j * P:(j + 1) * P], ident[:, :])
                            t.then_inc(sem("latT_psum"), 1)
                            wait_value(pe, sem("latT"), n + 1)
                            for j, bank in enumerate((Q0, Q1)):
                                w = H * HD // 2
                                for k in range(2):
                                    m = pe.matmul(bank[:, 0:w], latT[b][:, k, :], w_q[:, k, j * w:(j + 1) * w],
                                                  start=(k == 0), stop=(k == 1))
                            m.then_inc(sem("q_psum"), 1)
                            for j, bank in enumerate((KV0, KV1)):
                                m = pe.matmul(bank[:, :], latT[b][:, 2, :], w_kv[:, j * BANK:(j + 1) * BANK], start=True, stop=True)
                            m.then_inc(sem("kv_psum"), 1)

                        two_stage_loop(pe, T, latents, heads)

                    @block.scalar
                    def _(act):
                        act.wait_ge(sem("bias_psum"), 1)
                        act.activation(bias_gu[:, :], banks[4][:, :], ACT.Copy).then_inc(sem("bias_read"), 1)
                        act.wait_ge(sem("reduced"), 2)
                        act.activation(cc[:, :, 0:HALF], red, ACT.Sin).then_inc(sem("angles"), 1)
                        act.activation(cc[:, :, HALF:ROPE], red, ACT.Sin).then_inc(sem("angles"), 1)
                        act.activation(sn[:, :, 0:HALF], ang, ACT.Sin, scale=-1.0).then_inc(sem("angles"), 1)
                        act.activation(sn[:, :, HALF:ROPE], ang, ACT.Sin).then_inc(sem("angles"), 1)

                        def norm_x(n, b):
                            wait_value(act, sem(f"x{b}"), 8 * n + (16 - 8 * b))
                            act.activation(junk, xt[b], ACT.Square, scale=float(D) ** -0.5, accum_out=ms[b]).then_inc(sem("a_ms"), 1)
                            wait_value(act, sem("a_ms"), n + 1)
                            act.activation(rms[b], ms[b], ACT.Sqrt, bias=eps[:, :]).then_inc(sem("rms"), 1)
                            wait_value(act, sem("xT_psum"), n + 1)
                            if not (isinstance(n, int) and n == 0):
                                wait_value(act, sem("hts_kept"), n)
                            act.activation(hts[b][:, 0:4, :].rearrange("p k t -> p (k t)"), TP0[:, :], ACT.Copy).then_inc(sem("hts_ready"), 1)

                        def norm_heads(n, b):
                            wait_value(act, sem("lat_psum"), n + 1)
                            for j, (lo, hi) in enumerate(((0, QL), (QL, QL + KL), (QL + KL, LAT))):
                                act.activation(junk[:, lo:hi], BL[:, lo:hi], ACT.Square, scale=float(hi - lo) ** -0.5,
                                               accum_out=ms3[:, j:j + 1]).then_inc(sem("a_ms3"), 1)
                            wait_value(act, sem("a_ms3"), 3 * n + 3)
                            act.activation(rms3, ms3, ACT.Sqrt, bias=eps[:, :]).then_inc(sem("rms3"), 1)
                            wait_value(act, sem("q_psum"), n + 1)
                            for j, bank in enumerate((Q0, Q1)):
                                act.activation(sq_q[:, 4 * j:4 * j + 4, :].rearrange("p h d -> p (h d)"), bank[:, 0:H * HD // 2],
                                               ACT.Square, scale=float(HD) ** -0.5).then_inc(sem("sq"), 1)
                            wait_value(act, sem("kv_psum"), n + 1)
                            for j, bank in enumerate((KV0, KV1)):
                                kv = bank[:, :].rearrange("p (h d) -> p h d", d=NOPE + V)
                                act.activation(sq_k[:, 4 * j:4 * j + 4, :], kv[:, :, 0:NOPE],
                                               ACT.Square, scale=float(NOPE) ** -0.5).then_inc(sem("sq"), 1)
                            for j, bank in enumerate((KV0, KV1)):
                                kv = bank[:, :].rearrange("p (h d) -> p h d", d=NOPE + V)
                                v = act.activation(v_full[:, bass.ds(n, 1), 4 * j:4 * j + 4, :].rearrange("p o h d -> p (o h) d"),
                                                   kv[:, :, NOPE:NOPE + V], ACT.Copy)
                            v.then_inc(sem("v_kept"), 1)
                            wait_value(act, sem("msh"), 2 * n + 2)
                            act.activation(rmsh, msh, ACT.Sqrt, bias=eps[:, :]).then_inc(sem("rmsh"), 1)

                        two_stage_loop(act, T, norm_x, norm_heads)

                    @block.vector
                    def _(dve):
                        dve.wait_ge(sem("bias_psum"), 1)
                        dve.tensor_copy(bias_dn[:, :], banks[5][:, 0:E * K]).then_inc(sem("bias_read"), 1)
                        two_pi = 2.0 * np.pi
                        c1 = 6.28125
                        c2 = float(np.float32(np.round((two_pi - c1) * 2.0 ** 20) / 2.0 ** 20))
                        c3 = float(np.float32(two_pi - c1 - c2))
                        magic = 1.5 * 2.0 ** 23
                        pi_in = float(np.nextafter(np.float32(np.pi), np.float32(0)))
                        dve.wait_ge(sem("pos"), 16)
                        dve.wait_ge(sem("pc"), 2 + HALF)
                        dve.wait_ge(always, 1)
                        dve.tensor_copy(pos_f, pos_i).then_inc(sem("v"), 1)
                        dve.wait_ge(sem("v"), 1)
                        dve.tensor_tensor(ang, pos_f.unsqueeze(2).broadcast_to([P, T, HALF]),
                                          inv.unsqueeze(1).broadcast_to([P, T, HALF]), ALU.mult).then_inc(sem("v"), 1)
                        dve.wait_ge(sem("v"), 2)
                        dve.tensor_scalar(turns, ang, 1.0 / two_pi, None, ALU.mult).then_inc(sem("v"), 1)
                        dve.wait_ge(sem("v"), 3)
                        dve.tensor_scalar(turns_c, turns, 0.25, magic, ALU.add, ALU.add).then_inc(sem("v"), 1)
                        dve.tensor_copy(ang_c, ang).then_inc(sem("v"), 1)
                        dve.wait_ge(sem("v"), 5)
                        dve.tensor_scalar(turns, turns, magic, None, ALU.add).then_inc(sem("v"), 1)
                        dve.wait_ge(sem("v"), 6)
                        dve.tensor_scalar(turns, turns, -magic, None, ALU.add).then_inc(sem("v"), 1)
                        dve.tensor_scalar(turns_c, turns_c, -magic, None, ALU.add).then_inc(sem("v"), 1)
                        v = 8
                        for part in (c1, c2, c3):
                            dve.wait_ge(sem("v"), v)
                            dve.scalar_tensor_tensor(ang, turns, -part, ang, ALU.mult, ALU.add).then_inc(sem("v"), 1)
                            dve.scalar_tensor_tensor(ang_c, turns_c, -part, ang_c, ALU.mult, ALU.add).then_inc(sem("v"), 1)
                            v += 2
                        dve.wait_ge(sem("v"), v)
                        dve.tensor_scalar(ang_c, ang_c, float(np.float32(np.pi / 2)), None, ALU.add).then_inc(sem("v"), 1)
                        dve.wait_ge(sem("v"), v + 1)
                        dve.tensor_scalar(red, ang_c, pi_in, -pi_in, ALU.min, ALU.max).then_inc(sem("reduced"), 1)
                        dve.tensor_scalar(ang, ang, pi_in, -pi_in, ALU.min, ALU.max).then_inc(sem("reduced"), 1)

                        def norm_x(n, b):
                            wait_value(dve, sem("rms"), n + 1)
                            dve.reciprocal(rstd[b], rms[b]).then_inc(sem("v_rstd"), 1)
                            if isinstance(n, int) and n == 0:
                                dve.wait_ge(sem("gain"), 16)
                                dve.wait_ge(sem("angles"), 4)
                                dve.wait_ge(sem("g_small"), 80)
                            wait_value(dve, sem("v_rstd"), n + 1)
                            dve.scalar_tensor_tensor(xn[b], xt[b], rstd[b], gain_row[:, :], ALU.mult, ALU.mult).then_inc(sem("xn_ready"), 1)
                            wait_value(dve, sem("xT_psum"), n + 1)
                            if not (isinstance(n, int) and n == 0):
                                wait_value(dve, sem("hts_kept"), n)
                            dve.tensor_copy(hts[b][:, 4:8, :].rearrange("p k t -> p (k t)"), TP1[:, :]).then_inc(sem("hts_ready"), 1)

                        def norm_heads(n, b):
                            wait_value(dve, sem("rms3"), n + 1)
                            dve.reciprocal(rs3, rms3).then_inc(sem("v_rs3"), 1)
                            if isinstance(n, int) and n == T - 1:
                                dve.wait_ge(sem("rotated"), n - 1)
                            wait_value(dve, sem("v_rs3"), n + 1)
                            dve.tensor_scalar(latn[b][:, 0:QL], BL[:, 0:QL], rs3[:, 0:1], None, ALU.mult)
                            dve.scalar_tensor_tensor(krn[b], BL[:, QL + KL:LAT], rs3[:, 2:3], g_kr, ALU.mult, ALU.mult)
                            dve.tensor_scalar(latn[b][:, QL:QL + KL], BL[:, QL:QL + KL], rs3[:, 1:2], None, ALU.mult).then_inc(sem("latn"), 1)
                            wait_value(dve, sem("latT_psum"), n + 1)
                            dve.tensor_tensor(latT[b], BT[:, 0:3 * P].rearrange("p (j t) -> p j t", t=P),
                                              g_lat3.unsqueeze(2).broadcast_to([P, 3, P]), ALU.mult).then_inc(sem("latT"), 1)
                            wait_value(dve, sem("sq"), 4 * n + 4)
                            dve.tensor_reduce(msh[:, 0:H], sq_q, AX.X, ALU.add).then_inc(sem("msh"), 1)
                            dve.tensor_reduce(msh[:, H:2 * H], sq_k, AX.X, ALU.add).then_inc(sem("msh"), 1)
                            wait_value(dve, sem("rmsh"), n + 1)
                            dve.reciprocal(rsh, rmsh).then_inc(sem("v_rsh"), 1)
                            wait_value(dve, sem("v_rsh"), n + 1)
                            for j, bank in enumerate((Q0, Q1)):
                                m = dve.tensor_tensor(q_tmp[b][:, 4 * j:4 * j + 4, :],
                                                      bank[:, 0:H * HD // 2].rearrange("p (h d) -> p h d", d=HD),
                                                      rsh[:, 4 * j:4 * j + 4].unsqueeze(2).broadcast_to([P, 4, HD]), ALU.mult)
                                if j:
                                    m.then_inc(sem("q_tmp"), 1)
                            for j, bank in enumerate((KV0, KV1)):
                                kv = bank[:, :].rearrange("p (h d) -> p h d", d=NOPE + V)
                                m = dve.tensor_tensor(k_tmp[b][:, 4 * j:4 * j + 4, :], kv[:, :, 0:NOPE],
                                                      rsh[:, H + 4 * j:H + 4 * j + 4].unsqueeze(2).broadcast_to([P, 4, NOPE]), ALU.mult)
                                if j:
                                    m.then_inc(sem("k_tmp"), 1)

                        two_stage_loop(dve, T, norm_x, norm_heads)

        def pool_branch():
            ctx, sem = stage("pool")
            PAD = POOL_WINDOWS[-1]
            with ctx:
                w_u = view(arena_m, 0, K, POOL)
                w_mix = view(arena_m, 4096, G, C)
                scale_c = view(arena_m, 4608, G)
                inv_n = view(arena_m, 4640, PAD)
                pads = [view(arena_w, spare_w + j * (S + PAD), S + PAD) for j in range(3)]
                pooled = [view(arena_m, 5120 + 1024 * b, S) for b in (0, 1)]
                uT, sums = pads[0], pads[1:]
                with nc.Block() as block:
                    @block.sync
                    def _(sp):
                        sp.dma_start(w_u, w_in[:, LAT:LAT + POOL].rearrange("(k p) n -> p k n", p=P)).then_inc(sem("w_u"), 16)
                        sp.dma_start(w_mix, w_pool.rearrange("o g c d -> c (o g) d")).then_inc(sem("w_mix"), 16)
                        sp.dma_start(scale_c, pool_scale[0].rearrange("(g c) -> c g", c=C), allow_slow_non_contiguous=True).then_inc(sem("w_mix"), 16)

                    @block.gpsimd
                    def _(pool):
                        for j in range(3):
                            pool.memset(pads[j][:, 0:PAD], 0.0).then_inc(sem("consts"), 1)
                        for j in range(PAD):
                            pool.memset(inv_n[:, j:j + 1], 1.0 / (j + 1)).then_inc(sem("consts"), 1)

                    @block.tensor
                    def _(pe):
                        pe.wait_ge(sem("w_u"), 16)

                        def channels(g):
                            for h in range(2):
                                for k in range(K):
                                    m = pe.matmul(banks[4 * (g % 2) + h][:, :], w_u[:, k, g * C:(g + 1) * C],
                                                  hT[:, k, h * BANK:(h + 1) * BANK], start=(k == 0), stop=(k == K - 1))
                            m.then_inc(sem("u_psum"), 1)

                        channels(0)
                        for g in range(G):
                            if g + 1 < G:
                                if g >= 1:
                                    pe.wait_ge(sem("u_kept"), 2 * g)
                                channels(g + 1)
                            if g == 0:
                                pe.wait_ge(sem("w_mix"), 32)
                            pe.wait_ge(sem("pooled"), g + 1)
                            if g >= 2:
                                pe.wait_ge(sem("mixed"), 2 * (g - 1))
                            for h in range(2):
                                m = pe.matmul(banks[4 * (g % 2) + 2 + h][:, :], w_mix[:, g, :], pooled[g % 2][:, h * BANK:(h + 1) * BANK],
                                              start=True, stop=True)
                            m.then_inc(sem("mix_psum"), 1)

                    @block.scalar
                    def _(act):
                        def scaled(g):
                            act.wait_ge(sem("mix_psum"), g + 1)
                            if g == 0:
                                act.wait_ge(sem("w_mix"), 32)
                            for h in range(2):
                                act.activation(mixedT[:, g, h * BANK:(h + 1) * BANK], banks[4 * (g % 2) + 2 + h][:, :], ACT.Copy,
                                               scale=scale_c[:, g:g + 1]).then_inc(sem("mixed"), 1)
                        for g in range(G):
                            act.wait_ge(sem("u_psum"), g + 1)
                            if g:
                                act.wait_ge(sem("pooled"), g)
                            for h in range(2):
                                act.activation(uT[:, PAD + h * BANK:PAD + (h + 1) * BANK], banks[4 * (g % 2) + h][:, :],
                                               ACT.Copy).then_inc(sem("u_kept"), 1)
                            if g:
                                scaled(g - 1)
                        scaled(G - 1)

                    @block.vector
                    def _(dve):
                        dve.wait_ge(sem("consts"), 3 + PAD)
                        step = 0
                        for g, window in enumerate(POOL_WINDOWS):
                            dve.wait_ge(sem("u_kept"), 2 * g + 2)
                            if g >= 2:
                                dve.wait_ge(sem("mix_psum"), g - 1)
                            src, shift = uT, 1
                            while shift < window:
                                dst = sums[(shift.bit_length() - 1) % 2]
                                dve.tensor_tensor(dst[:, PAD:PAD + S], src[:, PAD:PAD + S], src[:, PAD - shift:PAD + S - shift],
                                                  ALU.add).then_inc(sem("sum"), 1)
                                step += 1
                                dve.wait_ge(sem("sum"), step)
                                src, shift = dst, shift * 2
                            dve.tensor_tensor(pooled[g % 2][:, 0:window], src[:, PAD:PAD + window], inv_n[:, 0:window],
                                              ALU.mult).then_inc(sem("sum"), 1)
                            step += 1
                            dve.scalar_tensor_tensor(pooled[g % 2][:, window:S], src[:, PAD + window:PAD + S], 1.0 / window,
                                                     uT[:, PAD + window:PAD + S], ALU.mult, ALU.subtract)
                            dve.wait_ge(sem("sum"), step)
                            dve.tensor_tensor(pooled[g % 2][:, 0:window], pooled[g % 2][:, 0:window], uT[:, PAD:PAD + window],
                                              ALU.subtract).then_inc(sem("pooled"), 1)

        def attend():
            ctx, sem = stage("att")
            with ctx:
                qTh = [view(arena_m, 1024 * b, S) for b in (0, 1)]
                kTh = [view(arena_m, 2048 + 1024 * b, S) for b in (0, 1)]
                prob = [view(arena_m, 4096 + 1024 * b, S) for b in (0, 1)]
                probT = [view(arena_m, 6144 + 1024 * b, T, P) for b in (0, 1)]
                head_words = T * (2 * HD + V)
                qst = [view(arena_w, spare_w + head_words * b, T, HD) for b in (0, 1)]
                kst = [view(arena_w, spare_w + head_words * b + T * HD, T, HD) for b in (0, 1)]
                vst = [view(arena_w, spare_w + head_words * b + 2 * T * HD, T, V) for b in (0, 1)]
                base = spare_w + 2 * head_words
                negmax = [view(arena_w, base + b, 1) for b in (0, 1)]
                total = [view(arena_w, base + 2 + b, 1) for b in (0, 1)]
                rtotal = [view(arena_w, base + 4 + b, 1) for b in (0, 1)]
                maskb = sb("a_mask", [P, P], BF16, ctx=ctx)
                identb = sb("a_ident", [P, P], BF16, ctx=ctx)
                SCALE = float(1.0 / np.sqrt(HD))
                score = [banks[0:2], banks[2:4]]
                turn = banks[4:6]
                obank = banks[6:8]
                AHEAD = 2

                with nc.Block() as block:
                    @block.gpsimd
                    def _(pool):
                        pool.memset(maskb[:, :], 0.0).then_inc(sem("c"), 1)
                        pool.wait_ge(sem("c"), 1)
                        pool.affine_select(out=maskb[:, :], in_=maskb[:, :], compare_op=ALU.is_ge, fill=NEG, base=0,
                                           pattern=[[-1, P]], channel_multiplier=1).then_inc(sem("consts"), 1)
                        pool.tensor_copy(identb[:, :], ident[:, :]).then_inc(sem("consts"), 1)

                        def fetch(h, b):
                            if not isinstance(h, int):
                                wait_value(pool, sem("o_psum"), 2 * h - 2)
                            pool.tensor_copy(qst[b], q_full[:, :, bass.ds(h, 1), :].rearrange("p t o d -> p t (o d)"))
                            pool.tensor_copy(kst[b], k_full[:, :, bass.ds(h, 1), :].rearrange("p t o d -> p t (o d)"))
                            pool.tensor_copy(vst[b], v_full[:, :, bass.ds(h, 1), :].rearrange("p t o d -> p t (o d)")
                                             ).then_inc(sem("fetched"), 1)
                        fetch(0, 0)
                        fetch(1, 1)
                        pair_loop(pool, H, fetch, first=2)

                    def fills(h, b):
                        return [(src, dst[b], half) for src, dst in ((qst[b], qTh), (kst[b], kTh)) for half in (0, 1)]

                    def head_loop(eng, start, body):
                        start()
                        with eng.Fori(0, HP - 1) as i:
                            for b in (0, 1):
                                body(2 * i + b, b, True)
                        body(H - 2, 0, True)
                        body(H - 1, 1, False)

                    @block.tensor
                    def _(pe):
                        def turn_head(h, b):
                            wait_value(pe, sem("fetched"), h + 1)
                            for j, (src, dst, half) in enumerate(fills(h, b)):
                                if j >= 2:
                                    wait_value(pe, sem("qk_kept"), 4 * h + (j - 1))
                                for t in range(4):
                                    m = pe.transpose(turn[half][0:HD, t * P:(t + 1) * P], src[:, 4 * half + t, :], ident[:, :])
                                m.then_inc(sem("qk_psum"), 1)

                        def scores(h, b, s):
                            if s == 0:
                                wait_value(pe, sem("qk_kept"), 4 * h + 4)
                            if not (isinstance(h, int) and h == 0 and s < AHEAD):
                                wait_value(pe, sem("exps"), T * h + (s - 1))
                            width = (s + 1) * P
                            for j in range(0, width, BANK):
                                w = min(BANK, width - j)
                                last = j + w == width
                                m = pe.matmul(score[s % 2][j // BANK][:, 0:w], qTh[b][0:HD, s * P:(s + 1) * P], kTh[b][0:HD, j:j + w],
                                              start=True, stop=not last, skip_group_check=True)
                            m = pe.matmul(score[s % 2][s // 4][:, w - P:w], identb[:, :], maskb[:, :], start=False, stop=True,
                                          skip_group_check=True)
                            m.then_inc(sem("scores"), 1)

                        def step(h, b, s, more):
                            if s + AHEAD < T:
                                scores(h, b, s + AHEAD)
                            elif more:
                                scores(h + 1, 1 - b, s + AHEAD - T)
                            if s == 4 and more:
                                wait_value(pe, sem("qk_kept"), 4 * h + 8)
                            wait_value(pe, sem("normed"), T * h + (s + 1))
                            for t in range(s + 1):
                                m = pe.transpose(turn[t // 4][:, (t % 4) * P:(t % 4 + 1) * P], prob[s % 2][:, t * P:(t + 1) * P], ident[:, :])
                                if t in (3, s):
                                    m.then_inc(sem("probT_psum"), 1)
                            wait_value(pe, sem("probT_kept"), 12 * h + sum(1 + (j > 3) for j in range(s + 1)))
                            for t in range(s + 1):
                                m = pe.matmul(obank[s // 4][b * V:(b + 1) * V, (s % 4) * P:(s % 4 + 1) * P], vst[b][:, t, :],
                                              probT[s % 2][:, t, :], start=(t == 0), stop=(t == s))
                            if s % 4 == 3:
                                m.then_inc(sem("o_psum"), 1)
                            if s == 3 and more:
                                turn_head(h + 1, 1 - b)

                        def start():
                            pe.wait_ge(sem("consts"), 2)
                            turn_head(0, 0)
                            scores(0, 0, 0)
                            scores(0, 0, 1)

                        def body(h, b, more):
                            for s in range(T):
                                step(h, b, s, more)
                        head_loop(pe, start, body)

                    @block.scalar
                    def _(act):
                        def keep_q(h, b):
                            for j, (src, dst, half) in enumerate(fills(h, b)):
                                wait_value(act, sem("qk_psum"), 4 * h + (j + 1))
                                act.activation(dst[0:HD, half * BANK:(half + 1) * BANK], turn[half][0:HD, :], ACT.Copy).then_inc(sem("qk_kept"), 1)

                        def exps(h, s):
                            wait_value(act, sem("maxes"), T * h + (s + 1))
                            n1 = min(s + 1, 4) * P
                            two = s >= 4
                            pair = score[s % 2]
                            if two:
                                act.activation(prob[s % 2][:, 0:BANK], pair[0][:, :], ACT.Exp, bias=negmax[s % 2], scale=SCALE,
                                               accum_out=total[s % 2]).then_inc(sem("t1"), 1)
                                act.activation(prob[s % 2][:, BANK:(s + 1) * P], pair[1][:, 0:(s - 3) * P], ACT.Exp, bias=negmax[s % 2],
                                               scale=SCALE, accum_out=total2[s % 2]).then_inc(sem("exps"), 1)
                            else:
                                act.activation(prob[s % 2][:, 0:n1], pair[0][:, 0:n1], ACT.Exp, bias=negmax[s % 2], scale=SCALE,
                                               accum_out=total[s % 2]).then_inc(sem("exps"), 1)

                        total2 = [view(arena_w, base + 6 + b, 1) for b in (0, 1)]

                        def step(h, b, s, more):
                            if s >= 4:
                                wait_value(act, sem("probT_psum"), 12 * h + sum(1 + (j > 3) for j in range(s + 1)))
                                act.activation(probT[s % 2][:, 4:s + 1, :].rearrange("p t q -> p (t q)"), turn[1][:, 0:(s - 3) * P],
                                               ACT.Copy).then_inc(sem("probT_kept"), 1)
                            if s + AHEAD < T:
                                exps(h, s + AHEAD)
                            elif more:
                                exps(h + 1, s + AHEAD - T)
                            if s % 4 == 3:
                                wait_value(act, sem("o_psum"), 2 * h + (s // 4 + 1))
                                half = s // 4
                                act.activation(att_rows(h, b)[:, half * BANK:(half + 1) * BANK], obank[half][b * V:(b + 1) * V, :],
                                               ACT.Copy).then_inc(sem("o_kept"), 1)
                            if s == 3 and more:
                                keep_q(h + 1, 1 - b)

                        def att_rows(h, b):
                            pair = h // 2 if isinstance(h, int) else att_pair[0]
                            return attnT[b * V:(b + 1) * V, bass.ds(pair, 1), :].rearrange("p o s -> p (o s)")

                        att_pair = [None]
                        keep_q(0, 0)
                        exps(0, 0)
                        exps(0, 1)
                        with act.Fori(0, HP - 1) as i:
                            att_pair[0] = i
                            for b in (0, 1):
                                for s in range(T):
                                    step(2 * i + b, b, s, True)
                        for b in (0, 1):
                            for s in range(T):
                                step(H - 2 + b, b, s, b == 0)

                    @block.vector
                    def _(dve):
                        mpair = [view(arena_w, base + 8 + 2 * b, 2) for b in (0, 1)]
                        total2 = [view(arena_w, base + 6 + b, 1) for b in (0, 1)]
                        tsum = [view(arena_w, base + 12 + b, 1) for b in (0, 1)]

                        def maxes(h, s):
                            wait_value(dve, sem("scores"), T * h + (s + 1))
                            pair = score[s % 2]
                            r = dve.tensor_reduce(mpair[s % 2][:, 0:1], pair[0][:, 0:min(s + 1, 4) * P], AX.X, ALU.max)
                            if s >= 4:
                                r = dve.tensor_reduce(mpair[s % 2][:, 1:2], pair[1][:, 0:(s - 3) * P], AX.X, ALU.max)
                            r.then_inc(sem("m"), 1)
                            wait_value(dve, sem("m"), T * h + (s + 1))
                            if s >= 4:
                                dve.tensor_scalar(negmax[s % 2], mpair[s % 2][:, 0:1], mpair[s % 2][:, 1:2], -SCALE, ALU.max,
                                                  ALU.mult).then_inc(sem("maxes"), 1)
                            else:
                                dve.tensor_scalar(negmax[s % 2], mpair[s % 2][:, 0:1], -SCALE, None, ALU.mult).then_inc(sem("maxes"), 1)

                        def step(h, b, s, more):
                            wait_value(dve, sem("exps"), T * h + (s + 1))
                            if s >= 4:
                                dve.tensor_tensor(tsum[s % 2], total[s % 2], total2[s % 2], ALU.add).then_inc(sem("d"), 1)
                                wait_value(dve, sem("d"), 4 * h + (s - 3))
                                dve.reciprocal(rtotal[s % 2], tsum[s % 2]).then_inc(sem("r"), 1)
                            else:
                                dve.reciprocal(rtotal[s % 2], total[s % 2]).then_inc(sem("r"), 1)
                            wait_value(dve, sem("r"), T * h + (s + 1))
                            dve.tensor_scalar(prob[s % 2][:, 0:(s + 1) * P], prob[s % 2][:, 0:(s + 1) * P], rtotal[s % 2], None,
                                              ALU.mult).then_inc(sem("normed"), 1)
                            wait_value(dve, sem("probT_psum"), 12 * h + (sum(1 + (j > 3) for j in range(s)) + 1))
                            n = min(s + 1, 4)
                            dve.tensor_copy(probT[s % 2][:, 0:n, :].rearrange("p t q -> p (t q)"), turn[0][:, 0:n * P]).then_inc(sem("probT_kept"), 1)
                            if s + AHEAD < T:
                                maxes(h, s + AHEAD)
                            elif more:
                                maxes(h + 1, s + AHEAD - T)

                        def start():
                            maxes(0, 0)
                            maxes(0, 1)

                        def body(h, b, more):
                            for s in range(T):
                                step(h, b, s, more)
                        head_loop(dve, start, body)

        def merge():
            ctx, sem = stage("merge")
            with ctx:
                WB = 8192
                wga = [view(arena_w, WB + 3072 * b, K, P) for b in (0, 1)]
                wgp = [view(arena_w, WB + 3072 * b + 1024, K, P) for b in (0, 1)]
                wya = [view(arena_w, WB + 3072 * b + 2048, KA, P) for b in (0, 1)]
                wyp = [view(arena_w, WB + 3072 * b + 2560, KO, P) for b in (0, 1)]
                sig = [[view(arena_w, WB + 6144 + 512 * (2 * n + j), BANK) for j in (0, 1)] for n in (0, 1)]
                prod = [[view(arena_w, WB + 8192 + 512 * (2 * n + j), BANK) for j in (0, 1)] for n in (0, 1)]
                with nc.Block() as block:
                    @block.sync
                    def _(sp):
                        def columns(lo, c):
                            if isinstance(c, int):
                                return slice(lo + c * P, lo + (c + 1) * P)
                            return bass.ds(c * P + lo, P)

                        def load(c, b):
                            s = sem(f"w{b}")
                            sp.dma_start(wga[b], w_in[:, columns(GATE_A, c)].rearrange("(k p) n -> p k n", p=P)).then_inc(s, 16)
                            sp.dma_start(wgp[b], w_in[:, columns(GATE_P, c)].rearrange("(k p) n -> p k n", p=P)).then_inc(s, 16)
                            sp.dma_start(wya[b], w_attn_out[:, columns(0, c)].rearrange("(k p) n -> p k n", p=P)).then_inc(s, 16)
                            sp.dma_start(wyp[b], w_pool_out[:, columns(0, c)].rearrange("(k p) n -> p k n", p=P)).then_inc(s, 16)
                        load(0, 0)
                        load(1, 1)
                        sp.dma_start(view(arena_w, 0, K, D), w_o.rearrange("(k p) n -> p k n", p=P)).then_inc(sem("w_o"), 16)
                        with sp.Fori(1, K // 2) as i:
                            for b in (0, 1):
                                wait_value(sp, sem("psum_full"), 4 * i + (2 * b - 2))
                                load(2 * i + b, b)
                        sp.wait_ge(sem("w_o"), 16)

                    @block.tensor
                    def _(pe):
                        def column(c, b):
                            wait_value(pe, sem(f"w{b}"), 32 * c + (64 - 32 * b))
                            for n in (0, 1):
                                ga, gp, ya, yp = banks[4 * n:4 * n + 4]
                                half = slice(n * BANK, (n + 1) * BANK)
                                if not (isinstance(c, int) and c == 0):
                                    wait_value(pe, sem("psum_read"), 2 * c + (n - 1))
                                for bank, w, src, kk in ((ga, wga, hT, K), (gp, wgp, hT, K), (ya, wya, attnT, KA), (yp, wyp, mixedT, KO)):
                                    for k in range(kk):
                                        m = pe.matmul(bank[:, :], w[b][:, k, :], src[:, k, half], start=(k == 0), stop=(k == kk - 1))
                                    if bank is gp:
                                        m.then_inc(sem("gates_psum"), 1)
                                m.then_inc(sem("psum_full"), 1)
                        column(0, 0)
                        with pe.Fori(0, K // 2 - 1) as i:
                            column(2 * i + 1, 1)
                            column(2 * i + 2, 0)
                        column(K - 1, 1)

                    @block.scalar
                    def _(act):
                        def column(c, b):
                            for n in (0, 1):
                                wait_value(act, sem("gates_psum"), 2 * c + (n + 1))
                                if not (isinstance(c, int) and c == 0):
                                    wait_value(act, sem("psum_read"), 2 * c + (n - 1))
                                for j in (0, 1):
                                    act.activation(sig[n][j], banks[4 * n + j][:, :], ACT.Sigmoid).then_inc(sem("sig"), 1)
                        column(0, 0)
                        with act.Fori(0, K // 2 - 1) as i:
                            column(2 * i + 1, 1)
                            column(2 * i + 2, 0)
                        column(K - 1, 1)

                    @block.vector
                    def _(dve):
                        def column(c, b):
                            for n in (0, 1):
                                wait_value(dve, sem("psum_full"), 2 * c + (n + 1))
                                wait_value(dve, sem("sig"), 4 * c + (2 * n + 2))
                                if not (isinstance(c, int) and c == 0):
                                    wait_value(dve, sem("merged"), 2 * c + (n - 1))
                                dve.tensor_tensor(prod[n][0], banks[4 * n + 2][:, :], sig[n][0], ALU.mult)
                                dve.tensor_tensor(prod[n][1], banks[4 * n + 3][:, :], sig[n][1], ALU.mult).then_inc(sem("psum_read"), 1)
                        column(0, 0)
                        with dve.Fori(0, K // 2 - 1) as i:
                            column(2 * i + 1, 1)
                            column(2 * i + 2, 0)
                        column(K - 1, 1)

                    @block.gpsimd
                    def _(pool):
                        def column(c, b):
                            for n in (0, 1):
                                wait_value(pool, sem("psum_read"), 2 * c + (n + 1))
                                pool.tensor_tensor(mT[:, bass.ds(c, 1), n * BANK:(n + 1) * BANK].rearrange("p o s -> p (o s)"),
                                                   prod[n][0], prod[n][1], ALU.add).then_inc(sem("merged"), 1)
                        pair_loop(pool, K, column)

        def route():
            ctx, sem = stage("route")
            with ctx:
                w_out = view(arena_w, 0, K, D)
                xt = [view(arena_a, D * b, D) for b in (0, 1)]
                x1 = [view(arena_a, D * (2 + b), D) for b in (0, 1)]
                h2 = [view(arena_a, D * (4 + b), D) for b in (0, 1)]
                junk = view(arena_a, D * 6, D)
                mts = [view(arena_h, D * b, K, P) for b in (0, 1)]
                h2T = [view(arena_h, D * (2 + b), K, P) for b in (0, 1)]
                w_r = view(arena_h, 4096, K, E)
                b_r = view(arena_h, 4352, E)
                zeros = view(arena_h, 4608, SLOTS // P).bitcast(I32)
                tok = view(arena_h, 5120, T).bitcast(I32)
                part = view(arena_h, 5130, 1)
                ms, rms, rstd = (view(arena_h, 5132 + j, 1) for j in range(3))
                logit = view(arena_h, 5152, E)
                top8 = view(arena_h, 5184, 8)
                idx8 = view(arena_h, 5192, 8).bitcast(U32)
                idxf = view(arena_h, 5200, TOP_K)
                onehot = view(arena_h, 5248, TOP_K, E)
                taken = view(arena_h, 5376, TOP_K, E)
                slot_e = view(arena_h, 5504, E)
                base = view(arena_h, 5536, E)
                destf = view(arena_h, 5568, TOP_K)
                dst = [view(arena_h, 5576 + 4 * b, TOP_K).bitcast(I32) for b in (0, 1)]
                tokb = [view(arena_h, 5584 + b, 1).bitcast(I32) for b in (0, 1)]
                top_all = view(arena_h, 5632, T, 8)
                expo = view(arena_h, 5696, T, TOP_K)
                esum, ersum = view(arena_h, 5728, T), view(arena_h, 5736, T)
                c_0, c_a, c_b = (view(arena_h, 5760 + 2 * E * j, 2, E) for j in range(3))
                nit, cnt = c_0[:, 0, :], c_0[:, 1, :]
                eid, before, chunk, count, lo, cap, row = (view(arena_h, 6000 + j, 1) for j in range(7))
                le, tmp, oh, first, shift_e = (view(arena_h, 6112 + E * j, E) for j in range(5))
                slot_all, e_all, row_all = (view(arena_h, 6272 + T * TOP_K * j, T, TOP_K) for j in range(3))
                oh_all = view(arena_h, 6400, T * TOP_K, E)
                fields = view(arena_h, 6016, ITEM_FIELDS)
                fields_i = view(arena_h, 6024, ITEM_FIELDS).bitcast(I32)
                start_e = view(arena_h, 6048, E)
                earlier = sb("r_earlier", [P, P], BF16, ctx=ctx)
                ones = sb("r_ones", [P, P], BF16, ctx=ctx)
                chosen = sb("r_chosen", [P, E], BF16, ctx=ctx)
                TB0, TB1, LG, RK = banks[4:8]
                with nc.Block() as block:
                    @block.sync
                    def _(sp):
                        sp.dma_start(gain_row[:, :], g_ffn[0].partition_broadcast(P)).then_inc(sem("gain"), 16)
                        for b in (0, 1):
                            sp.dma_start(xt[b], x2d[b * P:(b + 1) * P, :]).then_inc(sem(f"x{b}"), 16)
                        sp.dma_start(w_r, w_router[0].rearrange("(k p) n -> p k n", p=P)).then_inc(sem("w_r"), 16)
                        sp.dma_start(b_r, b_router[0].partition_broadcast(P)).then_inc(sem("w_r"), 16)
                        sp.wait_ge(sem("zeros"), 1)
                        sp.dma_start(list_dram.rearrange("(p s) o -> p (s o)", p=P), zeros).then_inc(sem("listed"), 16)

                        def store(n, b):
                            wait_value(sp, sem("h2_ready"), n + 1)
                            sp.dma_start(x1_dram[bass.ds(n * P, P), :], x1[b]).then_inc(sem("stored"), 16)
                            sp.dma_start(h2_dram[bass.ds(n * P, P), :], h2[b]).then_inc(sem("stored"), 16)
                            wait_value(sp, sem("stored"), 32 * n + 32)
                        with sp.Fori(0, T // 2 - 1) as i:
                            for b in (0, 1):
                                store(2 * i + b, b)
                                sp.dma_start(xt[b], x2d[bass.ds(i * (2 * P) + (2 + b) * P, P), :]).then_inc(sem(f"x{b}"), 16)
                        store(T - 2, 0)
                        store(T - 1, 1)
                        sp.wait_ge(sem("fields"), 1)
                        sp.dma_start(item_dram, fields_i[0:ITEM_ROWS, :]).then_inc(sem("table"), 16)
                        sp.wait_ge(sem("table"), 16)
                        sp.dma_start(items[:, :], item_dram.rearrange("(o i) f -> o (i f)", o=1)).then_inc(sem("table"), 16)
                        sp.wait_ge(sem("table"), 32)

                    @block.gpsimd
                    def _(pool):
                        pool.memset(zeros, 0).then_inc(sem("zeros"), 1)
                        pool.iota(tok, pattern=[[P, T]], base=0, channel_multiplier=1).then_inc(sem("consts"), 1)
                        pool.iota(part, pattern=[[1, 1]], base=0, channel_multiplier=1,
                                  allow_small_or_imprecise_dtypes=True).then_inc(sem("consts"), 1)
                        pool.memset(ones[:, :], 1.0).then_inc(sem("consts"), 1)
                        pool.memset(earlier[:, :], 1.0).then_inc(sem("pc"), 1)
                        pool.wait_ge(sem("pc"), 1)
                        pool.affine_select(out=earlier[:, :], in_=earlier[:, :], compare_op=ALU.is_gt, fill=0.0, base=0,
                                           pattern=[[1, P]], channel_multiplier=-1).then_inc(sem("consts"), 1)

                        def fetch(n, b):
                            if not (isinstance(n, int) and n == 0):
                                wait_value(pool, sem("x1_psum"), n)
                            pool.tensor_copy(mts[b], mT[:, :, bass.ds(n * P, P)]).then_inc(sem("fetched"), 1)
                            if isinstance(n, int) and n == 0:
                                pool.wait_ge(sem("listed"), 16)
                                pool.wait_ge(sem("consts"), 4)

                        def scatter(n, b):
                            pool.tensor_copy(tokb[b], tok[:, bass.ds(n, 1)]).then_inc(sem("tokb"), 1)
                            wait_value(pool, sem("dst"), n + 1)
                            wait_value(pool, sem("tokb"), n + 1)
                            for j in range(TOP_K):
                                pool.indirect_dma_start(list_dram, bass.IndirectOffsetOnAxis(dst[b][:, j:j + 1], 0), tokb[b], None
                                                        ).then_inc(sem("scattered"), 16)
                            wait_value(pool, sem("scattered"), 64 * n + 64)
                        two_stage_loop(pool, T, fetch, scatter)

                    @block.tensor
                    def _(pe):
                        def project(n, b):
                            wait_value(pe, sem("fetched"), n + 1)
                            for j in (0, 1):
                                for k in range(K):
                                    m = pe.matmul(banks[2 * b + j][:, :], mts[b][:, k, :], w_out[:, k, j * BANK:(j + 1) * BANK],
                                                  start=(k == 0), stop=(k == K - 1))
                            m.then_inc(sem("x1_psum"), 1)

                        def router(n, b):
                            wait_value(pe, sem("h2_ready"), n + 1)
                            for k in range(K):
                                m = pe.transpose((TB0, TB1)[k // 4][:, (k % 4) * P:(k % 4 + 1) * P], h2[b][:, k * P:(k + 1) * P], ident[:, :])
                            m.then_inc(sem("h2T_psum"), 1)
                            wait_value(pe, sem("h2T"), 2 * n + 2)
                            for k in range(K):
                                m = pe.matmul(LG[:, 0:E], h2T[b][:, k, :], w_r[:, k, :], start=(k == 0), stop=(k == K - 1))
                            m.then_inc(sem("logits"), 1)
                            wait_value(pe, sem("chosen"), n + 1)
                            pe.matmul(RK[:, 0:E], earlier[:, :], chosen[:, :], start=True, stop=True)
                            pe.matmul(RK[:, E:2 * E], ones[:, :], chosen[:, :], start=True, stop=True).then_inc(sem("ranks"), 1)

                        pe.wait_ge(sem("w_r"), 32)
                        pe.wait_ge(sem("consts"), 4)
                        two_stage_loop(pe, T, project, router)

                    @block.scalar
                    def _(act):
                        def norm(n, b):
                            wait_value(act, sem("x1_sum"), n + 1)
                            act.activation(junk, x1[b], ACT.Square, scale=float(D) ** -0.5, accum_out=ms).then_inc(sem("ms"), 1)
                            wait_value(act, sem("ms"), n + 1)
                            act.activation(rms, ms, ACT.Sqrt, bias=eps[:, :]).then_inc(sem("rms"), 1)

                        def keep(n, b):
                            wait_value(act, sem("h2T_psum"), n + 1)
                            act.activation(h2T[b][:, 0:4, :].rearrange("p k t -> p (k t)"), TB0[:, :], ACT.Copy).then_inc(sem("h2T"), 1)
                        two_stage_loop(act, T, norm, keep)
                        act.wait_ge(sem("shifted"), 1)
                        act.activation(expo, expo, ACT.Exp).then_inc(sem("expo"), 1)

                    @block.vector
                    def _(dve):
                        done = [0]

                        def then(instruction):
                            instruction.then_inc(sem("chain"), 1)
                            done[0] += 1
                            dve.wait_ge(sem("chain"), done[0])

                        dve.wait_ge(sem("w_r"), 32)
                        dve.wait_ge(sem("gain"), 16)
                        then(dve.tensor_scalar(start_e, iota_e[:, :], float(S), None, ALU.mult))
                        then(dve.tensor_copy(base, start_e))

                        def norm(n, b):
                            wait_value(dve, sem("x1_psum"), n + 1)
                            wait_value(dve, sem(f"x{b}"), 8 * n + (16 - 8 * b))
                            for j in (0, 1):
                                half = slice(j * BANK, (j + 1) * BANK)
                                m = dve.tensor_tensor(x1[b][:, half], banks[2 * b + j][:, :], xt[b][:, half], ALU.add)
                            m.then_inc(sem("x1_sum"), 1)
                            wait_value(dve, sem("rms"), n + 1)
                            dve.reciprocal(rstd, rms).then_inc(sem("rstd"), 1)
                            wait_value(dve, sem("rstd"), n + 1)
                            dve.scalar_tensor_tensor(h2[b], x1[b], rstd, gain_row[:, :], ALU.mult, ALU.mult).then_inc(sem("h2_ready"), 1)

                        def choose(n, b):
                            steps = 7

                            def step(j, instruction):
                                instruction.then_inc(sem("v"), 1)
                                wait_value(dve, sem("v"), steps * n + (j + 1))
                            wait_value(dve, sem("h2T_psum"), n + 1)
                            dve.tensor_copy(h2T[b][:, 4:8, :].rearrange("p k t -> p (k t)"), TB1[:, :]).then_inc(sem("h2T"), 1)
                            wait_value(dve, sem("logits"), n + 1)
                            step(0, dve.tensor_tensor(logit, LG[:, 0:E], b_r, ALU.add))
                            step(1, dve.max(top8, logit))
                            step(2, dve.max_index(idx8, top8, logit))
                            dve.tensor_copy(top_all[:, bass.ds(n, 1), :].rearrange("p o e -> p (o e)"), top8)
                            step(3, dve.tensor_copy(idxf, idx8[:, 0:TOP_K]))
                            step(4, dve.tensor_tensor(onehot, iota_e[:, :].unsqueeze(1).broadcast_to([P, TOP_K, E]),
                                                      idxf.unsqueeze(2).broadcast_to([P, TOP_K, E]), ALU.is_equal))
                            dve.tensor_reduce(chosen[:, :], onehot.rearrange("p k e -> p e k"), AX.X, ALU.max).then_inc(sem("chosen"), 1)
                            wait_value(dve, sem("ranks"), n + 1)
                            step(5, dve.tensor_tensor(slot_e, RK[:, 0:E], base, ALU.add))
                            dve.tensor_tensor(base, RK[:, E:2 * E], base, ALU.add).then_inc(sem("base"), 1)
                            step(6, dve.tensor_tensor(taken, onehot, slot_e.unsqueeze(1).broadcast_to([P, TOP_K, E]), ALU.mult))
                            dve.tensor_reduce(destf, taken, AX.X, ALU.add).then_inc(sem("destf"), 1)
                            wait_value(dve, sem("destf"), n + 1)
                            dve.tensor_copy(slot_all[:, bass.ds(n, 1), :].rearrange("p o k -> p (o k)"), destf)
                            dve.tensor_copy(e_all[:, bass.ds(n, 1), :].rearrange("p o k -> p (o k)"), idxf)
                            dve.tensor_copy(dst[b], destf).then_inc(sem("dst"), 1)

                        two_stage_loop(dve, T, norm, choose)

                        dve.wait_ge(sem("base"), T)
                        dve.tensor_tensor(expo, top_all[:, :, 0:TOP_K], top_all[:, :, 0:1].broadcast_to([P, T, TOP_K]),
                                          ALU.subtract).then_inc(sem("shifted"), 1)
                        dve.wait_ge(sem("expo"), 1)
                        then(dve.tensor_reduce(esum, expo, AX.X, ALU.add))
                        then(dve.reciprocal(ersum, esum))
                        then(dve.tensor_tensor(gates_all[:, :, :], expo, ersum.unsqueeze(2).broadcast_to([P, T, TOP_K]), ALU.mult))

                        dve.wait_ge(sem("consts"), 4)
                        then(dve.tensor_tensor(cnt, base, start_e, ALU.subtract))
                        then(dve.tensor_scalar(nit, cnt, 0.0, 1.0, ALU.mult, ALU.add))
                        for j in range(1, (S + WIDTH - 1) // WIDTH):
                            then(dve.scalar_tensor_tensor(nit, cnt, float(j * WIDTH), nit, ALU.is_gt, ALU.add))
                        src, other, shift = c_a, c_b, 1
                        then(dve.tensor_copy(c_a, c_0))
                        while shift < E:
                            dve.tensor_copy(other[:, :, 0:shift], src[:, :, 0:shift])
                            then(dve.tensor_tensor(other[:, :, shift:E], src[:, :, shift:E], src[:, :, 0:E - shift], ALU.add))
                            src, other, shift = other, src, 2 * shift
                        then(dve.tensor_tensor(first, src[:, 1, :], cnt, ALU.subtract))
                        then(dve.tensor_scalar(le, src[:, 0, :], part, None, ALU.is_le))
                        then(dve.tensor_reduce(eid, le, AX.X, ALU.add))
                        then(dve.tensor_scalar(eid, eid, float(E - 1), None, ALU.min))
                        then(dve.tensor_tensor(tmp, le, nit, ALU.mult))
                        then(dve.tensor_reduce(before, tmp, AX.X, ALU.add))
                        then(dve.tensor_tensor(chunk, part, before, ALU.subtract))
                        then(dve.tensor_scalar(oh, iota_e[:, :], eid, None, ALU.is_equal))
                        then(dve.tensor_tensor(tmp, oh, cnt, ALU.mult))
                        then(dve.tensor_reduce(count, tmp, AX.X, ALU.add))
                        then(dve.tensor_tensor(tmp, oh, first, ALU.mult))
                        then(dve.tensor_reduce(row, tmp, AX.X, ALU.add))
                        then(dve.tensor_scalar(cap, count, -float(WIDTH), 0.0, ALU.add, ALU.max))
                        then(dve.tensor_scalar(lo, chunk, float(WIDTH), 0.0, ALU.mult, ALU.max))
                        then(dve.tensor_tensor(lo, lo, cap, ALU.min))
                        dve.tensor_copy(fields[:, 0:1], eid)
                        dve.scalar_tensor_tensor(fields[:, 1:2], eid, float(S), lo, ALU.mult, ALU.add)
                        dve.tensor_scalar(fields[:, 2:3], count, float(WIDTH), None, ALU.min)
                        dve.tensor_tensor(fields[:, 4:5], row, lo, ALU.add)
                        then(dve.tensor_copy(fields[:, 3:4], src[:, 0, E - 1:E]))
                        dve.tensor_copy(fields_i, fields).then_inc(sem("fields"), 1)

                        then(dve.tensor_tensor(shift_e, first, start_e, ALU.subtract))
                        then(dve.tensor_tensor(oh_all, iota_e[:, :].unsqueeze(1).broadcast_to([P, T * TOP_K, E]),
                                               e_all.rearrange("p t k -> p (t k)").unsqueeze(2).broadcast_to([P, T * TOP_K, E]), ALU.is_equal))
                        then(dve.tensor_tensor(oh_all, oh_all, shift_e.unsqueeze(1).broadcast_to([P, T * TOP_K, E]), ALU.mult))
                        then(dve.tensor_reduce(row_all.rearrange("p t k -> p (t k)"), oh_all, AX.X, ALU.add))
                        then(dve.tensor_tensor(row_all, row_all, slot_all, ALU.add))
                        dve.tensor_copy(dest_all[:, :, :], row_all)

        def experts():
            ctx, sem = stage("ex")
            with ctx:
                CW = 2 * P
                CH = FF // CW
                wg = [view(arena_w, 2 * K * CW * c, K, CW) for c in range(CH)]
                wu = [view(arena_w, 2 * K * CW * c + K * CW, K, CW) for c in range(CH)]
                wd = [view(arena_w, 2 * K * FF + KF * CW * c, KF, CW) for c in range(D // CW)]
                REST = WIDTH - P
                xg = view(arena_a, 0, D)
                xg2 = view(arena_a, D, D)[0:REST, :]
                y_a = view(arena_a, 2 * D, D)
                y_b = view(arena_a, 3 * D, D)[0:REST, :]
                xT = view(arena_a, 4 * D, K, WIDTH)
                actT = view(arena_a, 4 * D + K * WIDTH, KF, WIDTH)
                gc, sg, gs, yT = ([view(arena_m, WIDTH * (2 * j + b), WIDTH) for b in (0, 1)] for j in range(4))
                uc = [view(arena_m, WIDTH * (8 + j), WIDTH) for j in range(3)]
                bias = view(arena_m, 11 * WIDTH, 3 * K)
                idx_a = view(arena_m, 11 * WIDTH + 32, 1).bitcast(I32)
                idx_b = view(arena_m, 11 * WIDTH + 33, 1).bitcast(I32)[0:REST, :]
                GU, TX, DN, YA, YB = banks[0:3], banks[3], banks[4:6], banks[6], banks[7]
                fill_bank = (TX, DN[0], DN[1], TX)

                def field(eng, i, f, lo, hi):
                    where = i * ITEM_FIELDS + f
                    return eng.value_load(items[0:1, bass.ds(where, 1)], min_val=lo, max_val=hi)

                def n_items(eng):
                    return field(eng, 0, 3, E, E + S * TOP_K // WIDTH)

                with nc.Block() as block:
                    @block.sync
                    def _(sp):
                        def load(i, first):
                            e = field(sp, i, 0, 0, E - 1)
                            up, dn = w_gate_up[bass.ds(e, 1)], w_down[bass.ds(e, 1)]
                            for c in range(CH):
                                if not first:
                                    wait_value(sp, sem("gu_psum"), KF * i + (2 * c + 2 - KF))
                                for w, at in ((wg, c * CW), (wu, FF + c * CW)):
                                    sp.dma_start(w[c], up[:, :, at:at + CW].rearrange("o (k p) n -> p (o k) n", p=P)).then_inc(sem(f"w_gu{c}"), 16)
                            for c in range(D // CW):
                                if not first:
                                    wait_value(sp, sem("dn_psum"), K * i + (2 * c + 2 - K))
                                sp.dma_start(wd[c], dn[:, :, c * CW:(c + 1) * CW].rearrange("o (k p) n -> p (o k) n", p=P)).then_inc(sem(f"w_dn{c}"), 16)
                        n = n_items(sp)
                        load(0, True)
                        with sp.Fori(1, n) as i:
                            load(i, False)
                        sp.dma_start(view(arena_h, 0, K, D), w_ple_gate.rearrange("(k p) n -> p k n", p=P)).then_inc(sem("ple"), 16)
                        sp.dma_start(view(arena_m, 4096, KP, D), w_ple.rearrange("(k p) n -> p k n", p=P)).then_inc(sem("ple"), 16)
                        sp.dma_start(gain_row[:, :], g_ple[0].partition_broadcast(P)).then_inc(sem("ple"), 16)
                        sp.wait_ge(sem("ple"), 48)

                    @block.gpsimd
                    def _(pool):
                        def gather(i):
                            slot = field(pool, i, 1, 0, SLOTS - WIDTH)
                            pool.dma_start(idx_a, list_dram[bass.ds(slot, P), :]).then_inc(sem("idx"), 16)
                            pool.dma_start(idx_b, list_dram[bass.ds(slot + P, REST), :]).then_inc(sem("idx"), 16)
                            wait_value(pool, sem("idx"), 32 * i + 32)
                            pool.indirect_dma_start(xg, None, h2_dram, bass.IndirectOffsetOnAxis(idx_a, 0)).then_inc(sem("xg"), 16)
                            pool.indirect_dma_start(xg2, None, h2_dram, bass.IndirectOffsetOnAxis(idx_b, 0)).then_inc(sem("xg"), 16)
                            wait_value(pool, sem("xg"), 32 * i + 32)
                        n = n_items(pool)
                        gather(0)
                        with pool.Fori(0, n) as i:
                            wait_value(pool, sem("x_psum"), 4 * i + 4)
                            gather(i + 1)

                    @block.tensor
                    def _(pe):
                        def turn_x(i):
                            wait_value(pe, sem("xg"), 32 * i + 32)
                            for j, bank in enumerate(fill_bank):
                                if j == 3:
                                    wait_value(pe, sem("xT_act"), 2 * i + 1)
                                for h in (0, 1):
                                    d = 2 * j + h
                                    pe.transpose(bank[:, h * WIDTH:h * WIDTH + P], xg[:, d * P:(d + 1) * P], ident[:, :])
                                    m = pe.transpose(bank[:, h * WIDTH + P:(h + 1) * WIDTH], xg2[:, d * P:(d + 1) * P], ident[0:REST, 0:REST])
                                m.then_inc(sem("x_psum"), 1)

                        def item(i, width):
                            wait_value(pe, sem("xT_act"), 2 * i + 2)
                            wait_value(pe, sem("xT_dve"), 2 * i + 2)
                            for f in range(KF):
                                c, at = f // 2, (f % 2) * P
                                if f % 2 == 0:
                                    wait_value(pe, sem(f"w_gu{c}"), 32 * i + 32)
                                if f >= 3:
                                    wait_value(pe, sem("gu_read"), KF * i + (f - 2))
                                for w, to in ((wg, 0), (wu, WIDTH)):
                                    for k in range(K):
                                        m = pe.matmul(GU[f % 3][:, to:to + width], w[c][:, k, at:at + P], xT[:, k, 0:width],
                                                      start=(k == 0), stop=(k == K - 1), skip_group_check=True)
                                m.then_inc(sem("gu_psum"), 1)
                            turn_x(i + 1)
                            wait_value(pe, sem("act"), KF * i + KF)
                            for d in range(K):
                                c, at = d // 2, (d % 2) * P
                                if d % 2 == 0:
                                    wait_value(pe, sem(f"w_dn{c}"), 16 * i + 16)
                                if d == 0:
                                    wait_value(pe, sem("xT_dve"), 2 * i + 3)
                                elif d == 1:
                                    wait_value(pe, sem("xT_act"), 2 * i + 4)
                                else:
                                    wait_value(pe, sem("yT"), K * i + (d - 1))
                                for k in range(KF):
                                    m = pe.matmul(DN[d % 2][:, 0:width], wd[c][:, k, at:at + P], actT[:, k, 0:width],
                                                  start=(k == 0), stop=(k == KF - 1))
                                m.then_inc(sem("dn_psum"), 1)
                                if d:
                                    turn_y(i, d - 1)
                            turn_y(i, K - 1)

                        def turn_y(i, d):
                            wait_value(pe, sem("yT"), K * i + (d + 1))
                            if d == 4:
                                wait_value(pe, sem("y_kept"), 4 * i + 2)
                            at = slice((d % 4) * P, (d % 4 + 1) * P)
                            pe.transpose(YA[:, at], yT[d % 2][:, 0:P], ident[:, :])
                            pe.transpose(YB[0:REST, at], yT[d % 2][:, P:WIDTH], ident[:, :]).then_inc(sem("y_psum"), 1)

                        def by_width(i, width, widths):
                            if len(widths) == 1:
                                item(i, widths[0])
                                return
                            with pe.If(width < widths[0] + 1):
                                item(i, widths[0])
                            with pe.Else():
                                by_width(i, width, widths[1:])

                        n = n_items(pe)
                        pe.wait_ge(sem("psum_set"), 5)
                        turn_x(0)
                        with pe.Fori(0, n) as i:
                            by_width(i, field(pe, i, 2, 0, WIDTH), WIDTHS)

                    @block.scalar
                    def _(act):
                        def keep_x(i):
                            for j in (0, 2):
                                wait_value(act, sem("x_psum"), 4 * i + (j + 1))
                                act.activation(xT[:, 2 * j:2 * j + 2, :].rearrange("p k t -> p (k t)"), fill_bank[j][:, 0:2 * WIDTH],
                                               ACT.Copy).then_inc(sem("xT_act"), 1)
                        n = n_items(act)
                        keep_x(0)
                        with act.Fori(0, n) as i:
                            for f in range(KF):
                                wait_value(act, sem("gc"), KF * i + (f + 1))
                                act.activation(sg[f % 2], gc[f % 2], ACT.Sigmoid, scale=SWIGLU_ALPHA).then_inc(sem("sg"), 1)
                            keep_x(i + 1)
                            for half in (0, 1):
                                wait_value(act, sem("y_psum"), K * i + 4 * (half + 1))
                                at = slice(half * BANK, (half + 1) * BANK)
                                act.activation(y_a[:, at], YA[:, :], ACT.Copy).then_inc(sem("y_kept"), 1)
                                act.activation(y_b[:, at], YB[0:REST, :], ACT.Copy).then_inc(sem("y_kept"), 1)
                            row = field(act, i, 4, 0, ROWS)
                            wait_value(act, sem("y_kept"), 4 * i + 4)
                            act.dma_start(y_dram[bass.ds(row, P), :], y_a).then_inc(sem("stored"), 16)
                            act.dma_start(y_dram[bass.ds(row + P, REST), :], y_b).then_inc(sem("stored"), 16)
                            wait_value(act, sem("stored"), 32 * i + 32)

                    @block.vector
                    def _(dve):
                        for bank in (*GU, *DN):
                            dve.memset(bank[:, :], 0.0).then_inc(sem("psum_set"), 1)

                        def keep_x(i):
                            for j in (1, 3):
                                wait_value(dve, sem("x_psum"), 4 * i + (j + 1))
                                dve.tensor_copy(xT[:, 2 * j:2 * j + 2, :].rearrange("p k t -> p (k t)"), fill_bank[j][:, 0:2 * WIDTH]
                                                ).then_inc(sem("xT_dve"), 1)
                        n = n_items(dve)
                        keep_x(0)
                        with dve.Fori(0, n) as i:
                            e = field(dve, i, 0, 0, E - 1)
                            dve.tensor_copy(bias[:, 0:KF], bias_gu[:, bass.ds(e * (2 * KF), KF)])
                            dve.tensor_scalar(bias[:, KF:2 * KF], bias_gu[:, bass.ds(e * (2 * KF) + KF, KF)], 1.0, None, ALU.add)
                            dve.tensor_copy(bias[:, 2 * KF:2 * KF + K], bias_dn[:, bass.ds(e * K, K)]).then_inc(sem("bias"), 1)
                            wait_value(dve, sem("bias"), i + 1)

                            def swiglu(f):
                                wait_value(dve, sem("sg"), KF * i + (f + 1))
                                dve.tensor_tensor(gs[f % 2], gc[f % 2], sg[f % 2], ALU.mult).then_inc(sem("gs"), 1)
                                wait_value(dve, sem("gs"), KF * i + (f + 1))
                                dve.scalar_tensor_tensor(actT[:, f, :], uc[f % 3], 1.0 - SWIGLU_LIMIT, gs[f % 2], ALU.max, ALU.mult).then_inc(sem("act"), 1)

                            for f in range(KF):
                                wait_value(dve, sem("gu_psum"), KF * i + (f + 1))
                                bank = GU[f % 3]
                                dve.tensor_scalar(gc[f % 2], bank[:, 0:WIDTH], bias[:, f:f + 1], SWIGLU_LIMIT, ALU.add, ALU.min).then_inc(sem("gc"), 1)
                                dve.tensor_scalar(uc[f % 3], bank[:, WIDTH:2 * WIDTH], bias[:, KF + f:KF + f + 1], 1.0 + SWIGLU_LIMIT,
                                                  ALU.add, ALU.min).then_inc(sem("gu_read"), 1)
                                if f:
                                    swiglu(f - 1)
                            swiglu(KF - 1)
                            keep_x(i + 1)
                            for d in range(K):
                                wait_value(dve, sem("dn_psum"), K * i + (d + 1))
                                if d >= 2:
                                    wait_value(dve, sem("y_psum"), K * i + (d - 1))
                                dve.tensor_scalar(yT[d % 2], DN[d % 2][:, 0:WIDTH], bias[:, 2 * KF + d:2 * KF + d + 1], None, ALU.add
                                                  ).then_inc(sem("yT"), 1)
                            wait_value(dve, sem("yT"), K * i + K)

        def combine():
            ctx, sem = stage("comb")
            with ctx:
                w_gate = view(arena_h, 0, K, D)
                w_emb = view(arena_m, 4096, KP, D)
                yg = [[view(arena_w, D * (4 * b + j), D) for j in range(TOP_K)] for b in (0, 1)]
                x1, x2, xn, outt = ([view(arena_w, D * (8 + 2 * j + b), D) for b in (0, 1)] for j in range(4))
                xnT = [view(arena_w, D * (16 + b), K, P) for b in (0, 1)]
                pt = [view(arena_w, D * 18 + PLE * b, PLE) for b in (0, 1)]
                pT = [view(arena_w, D * 18 + PLE * (2 + b), KP, P) for b in (0, 1)]
                sig, junk = view(arena_w, D * 19, D), view(arena_w, D * 20, D)
                dst = [view(arena_w, D * 21 + 4 * b, TOP_K).bitcast(I32) for b in (0, 1)]
                gts = [view(arena_w, D * 21 + 8 + 4 * b, TOP_K) for b in (0, 1)]
                ms, rms, rstd = (view(arena_w, D * 21 + 16 + j, 1) for j in range(3))
                TB0, TB1, TP = banks[0:3]
                gate_bank, emb_bank = banks[4:6], banks[6:8]
                with nc.Block() as block:
                    @block.sync
                    def _(sp):
                        for b in (0, 1):
                            sp.dma_start(x1[b], x1_dram[b * P:(b + 1) * P, :]).then_inc(sem(f"x{b}"), 16)
                            sp.dma_start(pt[b], p2d[b * P:(b + 1) * P, :]).then_inc(sem(f"x{b}"), 16)

                        def store(n, b):
                            wait_value(sp, sem("out"), n + 1)
                            sp.dma_start(out2d[bass.ds(n * P, P), :], outt[b]).then_inc(sem("stored"), 16)
                            wait_value(sp, sem("stored"), 16 * n + 16)
                        with sp.Fori(0, T // 2 - 1) as i:
                            for b in (0, 1):
                                store(2 * i + b, b)
                                rows = bass.ds(i * (2 * P) + (2 + b) * P, P)
                                sp.dma_start(x1[b], x1_dram[rows, :]).then_inc(sem(f"x{b}"), 16)
                                sp.dma_start(pt[b], p2d[rows, :]).then_inc(sem(f"x{b}"), 16)
                        store(T - 2, 0)
                        store(T - 1, 1)

                    @block.gpsimd
                    def _(pool):
                        def gather(n, b):
                            if not isinstance(n, int):
                                wait_value(pool, sem("summed"), n - 1)
                            pool.tensor_copy(gts[b], gates_all[:, bass.ds(n, 1), :].rearrange("p o k -> p (o k)")).then_inc(sem("dst"), 1)
                            pool.tensor_copy(dst[b], dest_all[:, bass.ds(n, 1), :].rearrange("p o k -> p (o k)")).then_inc(sem("dst"), 1)
                            wait_value(pool, sem("dst"), 2 * n + 2)
                            for j in range(TOP_K):
                                pool.indirect_dma_start(yg[b][j], None, y_dram[0:ROWS, :], bass.IndirectOffsetOnAxis(dst[b][:, j:j + 1], 0)
                                                        ).then_inc(sem(f"y{b}"), 16)
                        gather(0, 0)
                        gather(1, 1)
                        pair_loop(pool, T, gather, first=2)

                    @block.vector
                    def _(dve):
                        def norm(n, b):
                            wait_value(dve, sem(f"x{b}"), 16 * n + (32 - 16 * b))
                            wait_value(dve, sem(f"y{b}"), 32 * n + (64 - 32 * b))
                            for j in range(TOP_K):
                                last = j == TOP_K - 1
                                dve.scalar_tensor_tensor(x2[b], yg[b][j], gts[b][:, j:j + 1], x1[b] if j == 0 else x2[b],
                                                         ALU.mult, ALU.add).then_inc(sem("summed" if last else "part"), 1)
                                if last:
                                    wait_value(dve, sem("summed"), n + 1)
                                else:
                                    wait_value(dve, sem("part"), 3 * n + (j + 1))
                            wait_value(dve, sem("rms"), n + 1)
                            dve.reciprocal(rstd, rms).then_inc(sem("rstd"), 1)
                            wait_value(dve, sem("rstd"), n + 1)
                            dve.scalar_tensor_tensor(xn[b], x2[b], rstd, gain_row[:, :], ALU.mult, ALU.mult).then_inc(sem("xn"), 1)

                        def finish(n, b):
                            wait_value(dve, sem("xnT_psum"), n + 1)
                            dve.tensor_copy(xnT[b][:, 4:8, :].rearrange("p k t -> p (k t)"), TB1[:, :]).then_inc(sem("xnT"), 1)
                            wait_value(dve, sem("sig"), 2 * n + 2)
                            wait_value(dve, sem("emb_psum"), n + 1)
                            for j in (0, 1):
                                half = slice(j * BANK, (j + 1) * BANK)
                                dve.tensor_tensor(outt[b][:, half], emb_bank[j][:, :], sig[:, half], ALU.mult).then_inc(sem("gated"), 1)
                            wait_value(dve, sem("gated"), 2 * n + 2)
                            dve.tensor_tensor(outt[b], outt[b], x2[b], ALU.add).then_inc(sem("out"), 1)
                        two_stage_loop(dve, T, norm, finish)

                    @block.scalar
                    def _(act):
                        def norm(n, b):
                            wait_value(act, sem("summed"), n + 1)
                            act.activation(junk, x2[b], ACT.Square, scale=float(D) ** -0.5, accum_out=ms).then_inc(sem("ms"), 1)
                            wait_value(act, sem("ms"), n + 1)
                            act.activation(rms, ms, ACT.Sqrt, bias=eps[:, :]).then_inc(sem("rms"), 1)

                        def gate(n, b):
                            wait_value(act, sem("xnT_psum"), n + 1)
                            act.activation(xnT[b][:, 0:4, :].rearrange("p k t -> p (k t)"), TB0[:, :], ACT.Copy).then_inc(sem("xnT"), 1)
                            act.activation(pT[b].rearrange("p k t -> p (k t)"), TP[:, 0:KP * P], ACT.Copy).then_inc(sem("xnT"), 1)
                            wait_value(act, sem("gate_psum"), n + 1)
                            for j in (0, 1):
                                act.activation(sig[:, j * BANK:(j + 1) * BANK], gate_bank[j][:, :], ACT.Sigmoid).then_inc(sem("sig"), 1)
                        two_stage_loop(act, T, norm, gate)

                    @block.tensor
                    def _(pe):
                        def tile(n, b):
                            wait_value(pe, sem("xn"), n + 1)
                            wait_value(pe, sem(f"x{b}"), 16 * n + (32 - 16 * b))
                            for k in range(K):
                                pe.transpose((TB0, TB1)[k // 4][:, (k % 4) * P:(k % 4 + 1) * P], xn[b][:, k * P:(k + 1) * P], ident[:, :])
                            for k in range(KP):
                                m = pe.transpose(TP[:, k * P:(k + 1) * P], pt[b][:, k * P:(k + 1) * P], ident[:, :])
                            m.then_inc(sem("xnT_psum"), 1)
                            wait_value(pe, sem("xnT"), 3 * n + 3)
                            for j in (0, 1):
                                for k in range(K):
                                    m = pe.matmul(gate_bank[j][:, :], xnT[b][:, k, :], w_gate[:, k, j * BANK:(j + 1) * BANK],
                                                  start=(k == 0), stop=(k == K - 1))
                            m.then_inc(sem("gate_psum"), 1)
                            for j in (0, 1):
                                for k in range(KP):
                                    m = pe.matmul(emb_bank[j][:, :], pT[b][:, k, :], w_emb[:, k, j * BANK:(j + 1) * BANK],
                                                  start=(k == 0), stop=(k == KP - 1))
                            m.then_inc(sem("emb_psum"), 1)
                        pair_loop(pe, T, tile)

        front()
        pool_branch()
        attend()
        merge()
        route()
        experts()
        combine()


INS = ["x", "p", "positions", "g_mix", "w_in", "g_q_lat", "w_q_b", "g_kv_lat", "w_kv_b", "g_q_head",
       "g_k_nope", "g_k_rope", "w_pool", "pool_scale", "w_attn_out", "w_pool_out", "w_o", "g_ffn",
       "w_router", "b_router", "w_gate_up", "b_gate_up", "w_down", "b_down", "g_ple", "w_ple_gate", "w_ple"]


def kernel(**inputs):
    import concourse.bacc as bacc
    from concourse.bass_utils import run_bass_kernel_spmd

    nc = bacc.Bacc("TRN2", target_bir_lowering=False, num_devices=1)
    arrays, args = {}, []
    for name in INS:
        a = np.ascontiguousarray(inputs[name])
        arrays[f"in_{name}_dram"] = a
        args.append(nc.dram_tensor(f"in_{name}_dram", a.shape, mybir.dt.from_np(a.dtype), kind="ExternalInput").ap())
    shape = inputs["x"].shape
    args.append(nc.dram_tensor("out_0_dram", shape, F32, kind="ExternalOutput").ap())
    build(nc, *args)
    r = run_bass_kernel_spmd(nc, [arrays], core_ids=[0])
    return r.results[0]["out_0_dram"]
```

```python
from contextlib import ExitStack

import numpy as np

import concourse.bass as bass
from concourse import mybir

ALU = mybir.AluOpType
ACT = mybir.ActivationFunctionType
AX = mybir.AxisListType
F32 = mybir.dt.float32
BF16 = mybir.dt.bfloat16
I32 = mybir.dt.int32
U32 = mybir.dt.uint32

P = 128
EPS = 1e-6
ROPE_THETA = 10000.0
SWIGLU_ALPHA = 1.702
SWIGLU_LIMIT = 7.0
TOP_K = 4
POOL_WINDOWS = (2, 4, 8, 16)
NEG = -1e30
BANK = 512

WIDTHS = (128, 136, 144, 152, 160, 192)
WIDTH = WIDTHS[-1]
ITEM_ROWS = 64
ITEM_FIELDS = 5


def ahead_loop(eng, tiles, ready, begin, finish):
    def tile(n, b):
        begin(n, b)
        ready(n + 1, 1 - b)
        finish(n, b)
    ready(0, 0)
    tile(0, 0)
    with eng.Fori(0, tiles // 2 - 1) as i:
        tile(2 * i + 1, 1)
        tile(2 * i + 2, 0)
    begin(tiles - 1, 1)
    finish(tiles - 1, 1)


def front_loop(eng, tiles, scale, turn, latent, latent_turned, heads):
    def tile(n, b, scales=True, turns=True, tail=True):
        latent(n, b)
        if scales:
            scale(n + 2, b)
        if turns:
            turn(n + 1, 1 - b)
        if tail:
            heads(n - 1, 1 - b)
        latent_turned(n, b)
    scale(0, 0)
    turn(0, 0)
    scale(1, 1)
    tile(0, 0, tail=False)
    with eng.Fori(0, tiles // 2 - 2) as i:
        tile(2 * i + 1, 1)
        tile(2 * i + 2, 0)
    tile(tiles - 3, 1)
    tile(tiles - 2, 0, scales=False)
    tile(tiles - 1, 1, scales=False, turns=False)
    heads(tiles - 1, 1)


def nothing(n, b):
    pass


def pair_loop(eng, tiles, body, first=0):
    with eng.Fori(first // 2, tiles // 2) as i:
        for b in (0, 1):
            body(2 * i + b, b)


def view(arena, start, *dims):
    flat = arena[:, start:start + int(np.prod(dims))]
    if len(dims) == 1:
        return flat
    names = "abc"[:len(dims)]
    return flat.rearrange(
        f"p ({' '.join(names)}) -> p {' '.join(names)}", **{n: d for n, d in zip(names, dims)})


def build(nc, x, p, positions, g_mix, w_in, g_q_lat, w_q_b, g_kv_lat, w_kv_b, g_q_head, g_k_nope,
          g_k_rope, w_pool, pool_scale, w_attn_out, w_pool_out, w_o, g_ffn, w_router, b_router,
          w_gate_up, b_gate_up, w_down, b_down, g_ple, w_ple_gate, w_ple, out):
    S, D = x.shape[1:]
    T = S // P
    K = D // P
    QL, KL = g_q_lat.shape[1], g_kv_lat.shape[1]
    HD = g_q_head.shape[1]
    NOPE, ROPE = g_k_nope.shape[1], g_k_rope.shape[1]
    HALF = ROPE // 2
    H = w_q_b.shape[2] // HD
    V = w_kv_b.shape[2] // H - NOPE
    LAT = QL + KL + ROPE
    G, C = w_pool.shape[1:3]
    POOL = G * C
    GATE_A = LAT + POOL
    GATE_P = GATE_A + D
    E = w_router.shape[2]
    FF = w_down.shape[2]
    KF = FF // P
    PLE = p.shape[3]
    KP = PLE // P
    AW = H * V
    KA, KO = AW // P, POOL // P
    HP = H // 2
    SLOTS = E * S
    ROWS = S * TOP_K

    x2d, out2d = x[0], out[0]
    w_in, w_q_b, w_kv_b, w_attn_out, w_pool_out, w_o = (
        a[0] for a in (w_in, w_q_b, w_kv_b, w_attn_out, w_pool_out, w_o))
    w_gate_up, w_down, w_ple_gate, w_ple, p2d = w_gate_up[0], w_down[0], w_ple_gate[0], w_ple[0], p[0, 0]

    x1_dram = nc.dram_tensor("x1_rows", [S, D], F32).ap()
    h2_dram = nc.dram_tensor("h2_rows", [S, D], F32).ap()
    list_dram = nc.dram_tensor("slot_tokens", [SLOTS, 1], I32).ap()
    y_dram = nc.dram_tensor("expert_rows", [S * TOP_K + WIDTH, D], F32).ap()
    item_dram = nc.dram_tensor("items", [ITEM_ROWS, ITEM_FIELDS], I32).ap()

    with ExitStack() as top:
        def sb(name, shape, dt=F32, ctx=top):
            return ctx.enter_context(nc.sbuf_tensor(name, shape, dt))

        arena_w = sb("arena_w", [P, 3 * 8192])
        arena_h = sb("arena_h", [P, 8192])
        arena_m = sb("arena_m", [P, 8192])
        arena_a = sb("arena_a", [P, 8192])
        ident = sb("ident", [P, P])
        gain_row = sb("gain_row", [P, D])
        eps = sb("eps", [P, 1])
        iota_e = sb("iota_e", [P, E])
        dest_all = sb("dest_all", [P, T, TOP_K], I32)
        gates_all = sb("gates_all", [P, T, TOP_K])
        items = sb("items_row", [1, ITEM_ROWS * ITEM_FIELDS], I32)
        bias_gu = sb("bias_gu", [P, E * 2 * KF])
        bias_dn = sb("bias_dn", [P, E * K])
        banks = [top.enter_context(nc.psum_tensor(f"bank{i}", [P, BANK], F32)) for i in range(8)]

        always = top.enter_context(nc.semaphore("always"))

        def wait_value(eng, sem, value):
            if not isinstance(value, int):
                value = eng.to_reg(value)
                eng.wait_ge(always, 1)
            eng.wait_ge(sem, value)

        hT = view(arena_h, 0, K, S)
        mT = view(arena_m, 0, K, S)
        attnT = view(arena_a, 0, KA, S)
        mixedT = view(arena_a, KA * S, KO, S)
        q_full = view(arena_w, 0, T, H, HD)
        k_full = view(arena_w, T * H * HD, T, H, HD)
        v_full = view(arena_w, 2 * T * H * HD, T, H, V)
        spare_w = 2 * T * H * HD + T * H * V

        front_sems = []

        def stage(name):
            ctx = ExitStack()
            sems = {}

            def sem(n):
                if n not in sems:
                    sems[n] = ctx.enter_context(nc.semaphore(f"{name}_{n}"))
                return sems[n]
            if name == "front":
                front_sems.append(sems)
            return ctx, sem

        w_u_late = view(arena_m, 0, K, POOL - 2 * C)
        w_u = ([view(arena_a, D * (6 + g), K, C) for g in (0, 1)] + [w_u_late[:, :, g * C:(g + 1) * C] for g in range(G - 2)])

        def pool_channels(pe, g):
            for h in range(2):
                for k in range(K):
                    m = pe.matmul(banks[4 * (g % 2) + h][:, :], w_u[g][:, k, :],
                                  hT[:, k, h * BANK:(h + 1) * BANK], start=(k == 0), stop=(k == K - 1))
            return m

        def front():
            ctx, sem = stage("front")
            with ctx:
                xt = [view(arena_a, D * b, D) for b in (0, 1)]
                xn = [view(arena_a, D * (2 + b), D) for b in (0, 1)]
                hts = [view(arena_a, D * (4 + b), K, P) for b in (0, 1)]
                latn = [view(arena_m, 400 * b, QL + KL) for b in (0, 1)]
                krn = [view(arena_m, 800 + 32 * b, ROPE) for b in (0, 1)]
                latT = [view(arena_m, 1024 + 512 * b, 3, P) for b in (0, 1)]
                q_tmp = [view(arena_m, 2048 + 768 * b, H, HD) for b in (0, 1)]
                k_tmp = [view(arena_m, 3584 + 512 * b, H, NOPE) for b in (0, 1)]
                sq_q = view(arena_m, 4608, H, HD)
                sq_k = view(arena_m, 5376, H, NOPE)
                qr = view(arena_m, 5888, H, ROPE)
                ra = view(arena_m, 6144, H, ROPE)
                rb = view(arena_m, 6400, H, ROPE)
                kra = view(arena_m, 6656, ROPE)
                krb = view(arena_m, 6688, ROPE)
                krr = view(arena_m, 6720, ROPE)
                g_lat3 = view(arena_m, 6752, 3)
                g_qh = view(arena_m, 6760, HD)
                g_kn = view(arena_m, 6856, NOPE)
                g_kr = view(arena_m, 6920, ROPE)
                stat = view(arena_m, 6960, 128)
                ms = [stat[:, b:b + 1] for b in (0, 1)]
                rms = [stat[:, 2 + b:3 + b] for b in (0, 1)]
                rstd = [stat[:, 4 + b:5 + b] for b in (0, 1)]
                ms3, rms3, rs3 = stat[:, 8:11], stat[:, 12:15], stat[:, 16:19]
                msh, rmsh, rsh = stat[:, 20:36], stat[:, 40:56], stat[:, 60:76]
                cc = view(arena_m, 7168, T, ROPE)
                sn = view(arena_m, 7168 + T * ROPE, T, ROPE)
                pos_i = stat.bitcast(I32)[:, 80:88]
                pos_f = stat[:, 90:98]
                inv = stat[:, 100:116]
                ang, turns, red = (view(arena_m, 2048 + 128 * j, T, HALF) for j in range(3))
                ang_c, turns_c = (view(arena_m, 2048 + 128 * j, T, HALF) for j in (3, 4))

                w_lat = view(arena_w, spare_w, K, LAT)
                w_q = view(arena_w, spare_w + K * LAT, 2, H * HD)
                w_kv = view(arena_w, spare_w + K * LAT + 2 * H * HD, H * (NOPE + V))
                behind = spare_w + K * LAT + 2 * H * HD + H * (NOPE + V)
                b_rows = view(arena_w, behind, 6, P)
                junk = view(arena_w, behind + 6 * P, D // 2).bitcast(BF16)

                TP0, TP1, BL0, BL1, Q0, Q1, KV0, KV1 = banks
                BL = (BL0, BL1)
                BT = TP0
                n_bias = (E * 2 * KF + E * K) // P

                with nc.Block() as block:
                    @block.sync
                    def _(sp):
                        sp.dma_start(pos_i, positions[0].rearrange("(t p) -> p t", p=P), allow_slow_non_contiguous=True).then_inc(sem("pos"), 16)
                        sp.dma_start(xt[0], x2d[0:P, :]).then_inc(sem("x0"), 16)
                        sp.dma_start(xt[1], x2d[P:2 * P, :]).then_inc(sem("x1"), 16)
                        sp.dma_start(gain_row[:, :], g_mix[0].partition_broadcast(P)).then_inc(sem("gain"), 16)
                        sp.dma_start(w_lat, w_in[:, 0:LAT].rearrange("(k p) n -> p k n", p=P)).then_inc(sem("w_lat"), 16)
                        sp.dma_start(w_q, w_q_b.rearrange("(k p) n -> p k n", p=P)).then_inc(sem("w_q"), 16)
                        sp.dma_start(w_kv, w_kv_b).then_inc(sem("w_kv"), 16)
                        for g in (0, 1):
                            sp.dma_start(w_u[g], w_in[:, LAT + g * C:LAT + (g + 1) * C].rearrange("(k p) n -> p k n", p=P)).then_inc(sem("w_u"), 16)
                        with sp.Fori(1, T // 2) as i:
                            for b in (0, 1):
                                wait_value(sp, sem("xn_ready"), 2 * i + (b - 1))
                                sp.dma_start(xt[b], x2d[bass.ds(i * (2 * P) + b * P, P), :]).then_inc(sem(f"x{b}"), 16)

                    @block.gpsimd
                    def _(pool):
                        pool.memset(eps[:, :], EPS).then_inc(always, 1)
                        pool.memset(ident[:, :], 0.0).then_inc(sem("pc"), 1)
                        pool.iota(iota_e[:, :], pattern=[[1, E]], base=0, channel_multiplier=0,
                                  allow_small_or_imprecise_dtypes=True).then_inc(sem("pc"), 1)
                        for j in range(HALF):
                            f = float(np.float32(ROPE_THETA) ** np.float32(-2 * j / ROPE))
                            pool.memset(inv[:, j:j + 1], f).then_inc(sem("pc"), 1)
                        pool.wait_ge(sem("pc"), 1)
                        pool.affine_select(out=ident[:, :], in_=ident[:, :], compare_op=ALU.not_equal, fill=1.0,
                                           base=0, pattern=[[-1, P]], channel_multiplier=1).then_inc(sem("ident"), 1)
                        pool.dma_start(g_lat3[:, 0:2], g_q_lat[0].rearrange("(k p) -> p k", p=P), allow_slow_non_contiguous=True).then_inc(sem("g_small"), 16)
                        pool.dma_start(g_lat3[:, 2:3], g_kv_lat[0].rearrange("(k p) -> p k", p=P), allow_slow_non_contiguous=True).then_inc(sem("g_small"), 16)
                        pool.dma_start(g_qh, g_q_head[0].partition_broadcast(P)).then_inc(sem("g_small"), 16)
                        pool.dma_start(g_kn, g_k_nope[0].partition_broadcast(P)).then_inc(sem("g_small"), 16)
                        pool.dma_start(g_kr, g_k_rope[0].partition_broadcast(P)).then_inc(sem("g_small"), 16)
                        pool.dma_start(b_rows[:, 0:4, :], b_gate_up[0].rearrange("e (f c) -> (e f) c", c=P)
                                       .rearrange("(j r) c -> r j c", r=P)).then_inc(sem("biases"), 16)
                        pool.dma_start(b_rows[:, 4:6, :], b_down[0].rearrange("e (f c) -> (e f) c", c=P)
                                       .rearrange("(j r) c -> r j c", r=P)).then_inc(sem("biases"), 16)
                        pool.wait_ge(sem("g_small"), 80)
                        pool.wait_ge(sem("angles"), 4)

                        pool.wait_ge(always, 1)
                        pool.sem_inc(sem("rotated"), 2)

                        def rotate(n, b):
                            wait_value(pool, sem("q_tmp"), n + 1)
                            gq = g_qh.unsqueeze(1)
                            pool.tensor_tensor(q_full[:, bass.ds(n, 1), :, 0:NOPE].rearrange("p o h d -> p (o h) d"),
                                               q_tmp[b][:, :, 0:NOPE],
                                               gq[:, :, 0:NOPE].broadcast_to([P, H, NOPE]), ALU.mult)
                            pool.tensor_tensor(qr, q_tmp[b][:, :, NOPE:HD],
                                               gq[:, :, NOPE:HD].broadcast_to([P, H, ROPE]), ALU.mult).then_inc(sem("pr"), 1)
                            c_n = cc[:, bass.ds(n, 1), :].broadcast_to([P, H, ROPE])
                            s_n = sn[:, bass.ds(n, 1), :].broadcast_to([P, H, ROPE])
                            wait_value(pool, sem("pr"), 4 * n + 1)
                            pool.tensor_tensor(ra, qr, c_n, ALU.mult).then_inc(sem("pr"), 1)
                            pool.tensor_tensor(rb[:, :, 0:HALF], qr[:, :, HALF:ROPE], s_n[:, :, 0:HALF], ALU.mult).then_inc(sem("pr"), 1)
                            pool.tensor_tensor(rb[:, :, HALF:ROPE], qr[:, :, 0:HALF], s_n[:, :, HALF:ROPE], ALU.mult).then_inc(sem("pr"), 1)
                            wait_value(pool, sem("pr"), 4 * n + 4)
                            pool.tensor_tensor(q_full[:, bass.ds(n, 1), :, NOPE:HD].rearrange("p o h d -> p (o h) d"),
                                               ra, rb, ALU.add)
                            wait_value(pool, sem("k_tmp"), n + 1)
                            pool.tensor_tensor(k_full[:, bass.ds(n, 1), :, 0:NOPE].rearrange("p o h d -> p (o h) d"),
                                               k_tmp[b], g_kn.unsqueeze(1).broadcast_to([P, H, NOPE]), ALU.mult).then_inc(sem("pk"), 1)
                            c_1 = cc[:, bass.ds(n, 1), :].rearrange("p o r -> p (o r)")
                            s_1 = sn[:, bass.ds(n, 1), :].rearrange("p o r -> p (o r)")
                            pool.tensor_tensor(kra, krn[b], c_1, ALU.mult).then_inc(sem("pk"), 1)
                            pool.tensor_tensor(krb[:, 0:HALF], krn[b][:, HALF:ROPE], s_1[:, 0:HALF], ALU.mult).then_inc(sem("pk"), 1)
                            pool.tensor_tensor(krb[:, HALF:ROPE], krn[b][:, 0:HALF], s_1[:, HALF:ROPE], ALU.mult).then_inc(sem("pk"), 1)
                            wait_value(pool, sem("pk"), 5 * n + 4)
                            pool.tensor_tensor(krr, kra, krb, ALU.add).then_inc(sem("pk"), 1)
                            wait_value(pool, sem("pk"), 5 * n + 5)
                            pool.tensor_copy(k_full[:, bass.ds(n, 1), :, NOPE:HD].rearrange("p o h d -> p (o h) d"),
                                             krr.unsqueeze(1).broadcast_to([P, H, ROPE])).then_inc(sem("rotated"), 1)

                        pair_loop(pool, T, rotate)

                    @block.tensor
                    def _(pe):
                        def latents(n, b):
                            wait_value(pe, sem("xn_ready"), n + 1)
                            for k in range(K):
                                t = pe.transpose((TP0, TP1)[k // 4][:, (k % 4) * P:(k % 4 + 1) * P],
                                                 xn[b][:, k * P:(k + 1) * P], ident[:, :])
                            t.then_inc(sem("xT_psum"), 1)
                            wait_value(pe, sem("hts_ready"), 2 * n + 2)
                            if isinstance(n, int) and n == 0:
                                pe.wait_ge(sem("w_lat"), 16)
                                pe.wait_ge(sem("w_q"), 16)
                                pe.wait_ge(sem("w_kv"), 16)
                            for k in range(K):
                                m = pe.matmul(BL[b][:, 0:LAT], hts[b][:, k, :], w_lat[:, k, :], start=(k == 0), stop=(k == K - 1))
                            m.then_inc(sem("lat_psum"), 1)

                        def heads(n, b):
                            wait_value(pe, sem("latn"), n + 1)
                            if isinstance(n, int) and n == T - 1:
                                pe.wait_ge(sem("hT_act"), T)
                            else:
                                wait_value(pe, sem("hT_act"), n + 2)
                            for j in range(3):
                                t = pe.transpose(BT[:, j * P:(j + 1) * P], latn[b][:, j * P:(j + 1) * P], ident[:, :])
                            t.then_inc(sem("latT_psum"), 1)
                            wait_value(pe, sem("latT"), n + 1)
                            for j, bank in enumerate((Q0, Q1)):
                                w = H * HD // 2
                                for k in range(2):
                                    m = pe.matmul(bank[:, 0:w], latT[b][:, k, :], w_q[:, k, j * w:(j + 1) * w],
                                                  start=(k == 0), stop=(k == 1))
                            m.then_inc(sem("q_psum"), 1)
                            for j, bank in enumerate((KV0, KV1)):
                                m = pe.matmul(bank[:, :], latT[b][:, 2, :], w_kv[:, j * BANK:(j + 1) * BANK], start=True, stop=True)
                            m.then_inc(sem("kv_psum"), 1)

                        pe.wait_ge(sem("ident"), 1)
                        front_loop(pe, T, nothing, latents, nothing, heads, nothing)

                        pe.wait_ge(sem("w_u"), 32)
                        pool_channels(pe, 0)
                        pe.wait_ge(sem("biases"), 32)
                        for j in range(n_bias):
                            t = pe.transpose(BL[j // 4][:, (j % 4) * P:(j % 4 + 1) * P], b_rows[:, j, :], ident[:, :])
                        t.then_inc(sem("bias_psum"), 1)

                    @block.scalar
                    def _(act):
                        def tables():
                            act.wait_ge(sem("reduced"), 2)
                            act.activation(cc[:, :, 0:HALF], red, ACT.Sin).then_inc(sem("angles"), 1)
                            act.activation(cc[:, :, HALF:ROPE], red, ACT.Sin).then_inc(sem("angles"), 1)
                            act.activation(sn[:, :, 0:HALF], ang, ACT.Sin, scale=-1.0).then_inc(sem("angles"), 1)
                            act.activation(sn[:, :, HALF:ROPE], ang, ACT.Sin).then_inc(sem("angles"), 1)

                        def scale(n, b):
                            wait_value(act, sem(f"x{b}"), 8 * n + (16 - 8 * b))
                            act.activation(junk, xt[b], ACT.Square, scale=float(D) ** -0.5, accum_out=ms[b]).then_inc(sem("a_ms"), 1)
                            wait_value(act, sem("a_ms"), n + 1)
                            act.activation(rms[b], ms[b], ACT.Sqrt, bias=eps[:, :]).then_inc(sem("rms"), 1)
                            if isinstance(n, int) and n == 1:
                                tables()

                        def turn(n, b):
                            wait_value(act, sem("xT_psum"), n + 1)
                            act.activation(hts[b][:, 0:4, :].rearrange("p k t -> p (k t)"), TP0[:, :], ACT.Copy).then_inc(sem("hts_ready"), 1)
                            act.activation(hT[:, 0:4, bass.ds(n * P, P)], TP0[:, :].rearrange("p (k t) -> p k t", t=P), ACT.Copy).then_inc(sem("hT_act"), 1)

                        def latent(n, b):
                            wait_value(act, sem("lat_psum"), n + 1)
                            for j, (lo, hi) in enumerate(((0, QL), (QL, QL + KL), (QL + KL, LAT))):
                                act.activation(junk[:, lo:hi], BL[b][:, lo:hi], ACT.Square, scale=float(hi - lo) ** -0.5,
                                               accum_out=ms3[:, j:j + 1]).then_inc(sem("a_ms3"), 1)
                            wait_value(act, sem("a_ms3"), 3 * n + 3)
                            act.activation(rms3, ms3, ACT.Sqrt, bias=eps[:, :]).then_inc(sem("rms3"), 1)

                        def heads(n, b):
                            wait_value(act, sem("q_psum"), n + 1)
                            for j, bank in enumerate((Q0, Q1)):
                                act.activation(sq_q[:, 4 * j:4 * j + 4, :].rearrange("p h d -> p (h d)"), bank[:, 0:H * HD // 2],
                                               ACT.Square, scale=float(HD) ** -0.5).then_inc(sem("sq"), 1)
                            wait_value(act, sem("kv_psum"), n + 1)
                            for j, bank in enumerate((KV0, KV1)):
                                kv = bank[:, :].rearrange("p (h d) -> p h d", d=NOPE + V)
                                act.activation(sq_k[:, 4 * j:4 * j + 4, :], kv[:, :, 0:NOPE],
                                               ACT.Square, scale=float(NOPE) ** -0.5).then_inc(sem("sq"), 1)
                            for j, bank in enumerate((KV0, KV1)):
                                kv = bank[:, :].rearrange("p (h d) -> p h d", d=NOPE + V)
                                act.activation(v_full[:, bass.ds(n, 1), 4 * j:4 * j + 4, :].rearrange("p o h d -> p (o h) d"),
                                               kv[:, :, NOPE:NOPE + V], ACT.Copy)
                            wait_value(act, sem("msh"), 2 * n + 2)
                            act.activation(rmsh, msh, ACT.Sqrt, bias=eps[:, :]).then_inc(sem("rmsh"), 1)

                        act.wait_ge(always, 1)
                        front_loop(act, T, scale, turn, latent, nothing, heads)
                        act.wait_ge(sem("bias_psum"), 1)
                        act.activation(bias_gu[:, :], BL0[:, :], ACT.Copy)

                    @block.vector
                    def _(dve):
                        two_pi = 2.0 * np.pi
                        c1 = 6.28125
                        c2 = float(np.float32(np.round((two_pi - c1) * 2.0 ** 20) / 2.0 ** 20))
                        c3 = float(np.float32(two_pi - c1 - c2))
                        magic = 1.5 * 2.0 ** 23
                        pi_in = float(np.nextafter(np.float32(np.pi), np.float32(0)))
                        dve.wait_ge(sem("pos"), 16)
                        dve.wait_ge(sem("pc"), 2 + HALF)
                        dve.wait_ge(always, 1)
                        dve.tensor_copy(pos_f, pos_i).then_inc(sem("v"), 1)
                        dve.wait_ge(sem("v"), 1)
                        dve.tensor_tensor(ang, pos_f.unsqueeze(2).broadcast_to([P, T, HALF]),
                                          inv.unsqueeze(1).broadcast_to([P, T, HALF]), ALU.mult).then_inc(sem("v"), 1)
                        dve.wait_ge(sem("v"), 2)
                        dve.tensor_scalar(turns, ang, 1.0 / two_pi, None, ALU.mult).then_inc(sem("v"), 1)
                        dve.wait_ge(sem("v"), 3)
                        dve.tensor_scalar(turns_c, turns, 0.25, magic, ALU.add, ALU.add).then_inc(sem("v"), 1)
                        dve.tensor_copy(ang_c, ang).then_inc(sem("v"), 1)
                        dve.wait_ge(sem("v"), 5)
                        dve.tensor_scalar(turns, turns, magic, None, ALU.add).then_inc(sem("v"), 1)
                        dve.wait_ge(sem("v"), 6)
                        dve.tensor_scalar(turns, turns, -magic, None, ALU.add).then_inc(sem("v"), 1)
                        dve.tensor_scalar(turns_c, turns_c, -magic, None, ALU.add).then_inc(sem("v"), 1)
                        v = 8
                        for part in (c1, c2, c3):
                            dve.wait_ge(sem("v"), v)
                            dve.scalar_tensor_tensor(ang, turns, -part, ang, ALU.mult, ALU.add).then_inc(sem("v"), 1)
                            dve.scalar_tensor_tensor(ang_c, turns_c, -part, ang_c, ALU.mult, ALU.add).then_inc(sem("v"), 1)
                            v += 2
                        dve.wait_ge(sem("v"), v)
                        dve.tensor_scalar(ang_c, ang_c, float(np.float32(np.pi / 2)), None, ALU.add).then_inc(sem("v"), 1)
                        dve.wait_ge(sem("v"), v + 1)
                        dve.tensor_scalar(red, ang_c, pi_in, -pi_in, ALU.min, ALU.max).then_inc(sem("reduced"), 1)
                        dve.tensor_scalar(ang, ang, pi_in, -pi_in, ALU.min, ALU.max).then_inc(sem("reduced"), 1)

                        def scale(n, b):
                            wait_value(dve, sem("rms"), n + 1)
                            dve.reciprocal(rstd[b], rms[b]).then_inc(sem("v_rstd"), 1)
                            if isinstance(n, int) and n == 0:
                                dve.wait_ge(sem("gain"), 16)
                            wait_value(dve, sem("v_rstd"), n + 1)
                            dve.scalar_tensor_tensor(xn[b], xt[b], rstd[b], gain_row[:, :], ALU.mult, ALU.mult).then_inc(sem("xn_ready"), 1)

                        def turn(n, b):
                            wait_value(dve, sem("xT_psum"), n + 1)
                            dve.tensor_copy(hts[b][:, 4:8, :].rearrange("p k t -> p (k t)"), TP1[:, :]).then_inc(sem("hts_ready"), 1)
                            dve.tensor_copy(hT[:, 4:8, bass.ds(n * P, P)], TP1[:, :].rearrange("p (k t) -> p k t", t=P))

                        def latent(n, b):
                            if isinstance(n, int) and n == 0:
                                dve.wait_ge(sem("angles"), 4)
                                dve.wait_ge(sem("g_small"), 80)
                            wait_value(dve, sem("rms3"), n + 1)
                            dve.reciprocal(rs3, rms3).then_inc(sem("v_rs3"), 1)
                            wait_value(dve, sem("rotated"), n + 1)
                            wait_value(dve, sem("v_rs3"), n + 1)
                            dve.tensor_scalar(latn[b][:, 0:QL], BL[b][:, 0:QL], rs3[:, 0:1], None, ALU.mult)
                            dve.scalar_tensor_tensor(krn[b], BL[b][:, QL + KL:LAT], rs3[:, 2:3], g_kr, ALU.mult, ALU.mult)
                            dve.tensor_scalar(latn[b][:, QL:QL + KL], BL[b][:, QL:QL + KL], rs3[:, 1:2], None, ALU.mult).then_inc(sem("latn"), 1)

                        def latent_turned(n, b):
                            wait_value(dve, sem("latT_psum"), n + 1)
                            dve.tensor_tensor(latT[b], BT[:, 0:3 * P].rearrange("p (j t) -> p j t", t=P),
                                              g_lat3.unsqueeze(2).broadcast_to([P, 3, P]), ALU.mult).then_inc(sem("latT"), 1)

                        def heads(n, b):
                            wait_value(dve, sem("sq"), 4 * n + 4)
                            dve.tensor_reduce(msh[:, 0:H], sq_q, AX.X, ALU.add).then_inc(sem("msh"), 1)
                            dve.tensor_reduce(msh[:, H:2 * H], sq_k, AX.X, ALU.add).then_inc(sem("msh"), 1)
                            wait_value(dve, sem("rmsh"), n + 1)
                            dve.reciprocal(rsh, rmsh).then_inc(sem("v_rsh"), 1)
                            wait_value(dve, sem("v_rsh"), n + 1)
                            for j, bank in enumerate((Q0, Q1)):
                                m = dve.tensor_tensor(q_tmp[b][:, 4 * j:4 * j + 4, :],
                                                      bank[:, 0:H * HD // 2].rearrange("p (h d) -> p h d", d=HD),
                                                      rsh[:, 4 * j:4 * j + 4].unsqueeze(2).broadcast_to([P, 4, HD]), ALU.mult)
                                if j:
                                    m.then_inc(sem("q_tmp"), 1)
                            for j, bank in enumerate((KV0, KV1)):
                                kv = bank[:, :].rearrange("p (h d) -> p h d", d=NOPE + V)
                                m = dve.tensor_tensor(k_tmp[b][:, 4 * j:4 * j + 4, :], kv[:, :, 0:NOPE],
                                                      rsh[:, H + 4 * j:H + 4 * j + 4].unsqueeze(2).broadcast_to([P, 4, NOPE]), ALU.mult)
                                if j:
                                    m.then_inc(sem("k_tmp"), 1)

                        front_loop(dve, T, scale, turn, latent, latent_turned, heads)
                        dve.wait_ge(sem("bias_psum"), 1)
                        dve.tensor_copy(bias_dn[:, :], BL1[:, 0:E * K])

        def pool_branch():
            ctx, sem = stage("pool")
            PAD = POOL_WINDOWS[-1]
            with ctx:
                w_mix = view(arena_m, 4096, G, C)
                scale_c = view(arena_m, 4608, G)
                inv_n = view(arena_m, 4640, PAD)
                pads = [view(arena_w, spare_w + j * (S + PAD), S + PAD) for j in range(3)]
                pooled = [view(arena_m, 5120 + 1024 * b, S) for b in (0, 1)]
                uT, sums = pads[0], pads[1:]
                with nc.Block() as block:
                    @block.sync
                    def _(sp):
                        sp.dma_start(w_u_late, w_in[:, LAT + 2 * C:LAT + POOL].rearrange("(k p) n -> p k n", p=P)).then_inc(sem("w_u"), 16)
                        sp.dma_start(w_mix, w_pool.rearrange("o g c d -> c (o g) d")).then_inc(sem("w_mix"), 16)
                        sp.dma_start(scale_c, pool_scale[0].rearrange("(g c) -> c g", c=C), allow_slow_non_contiguous=True).then_inc(sem("w_mix"), 16)

                    @block.gpsimd
                    def _(pool):
                        for s in front_sems[0].values():
                            pool.sem_clear(s)
                        for j in range(3):
                            pool.memset(pads[j][:, 0:PAD], 0.0).then_inc(sem("consts"), 1)
                        for j in range(PAD):
                            pool.memset(inv_n[:, j:j + 1], 1.0 / (j + 1)).then_inc(sem("consts"), 1)

                    @block.tensor
                    def _(pe):
                        for g in range(G):
                            if g + 1 < G:
                                if g >= 1:
                                    pe.wait_ge(sem("u_kept"), 2 * g)
                                if g == 1:
                                    pe.wait_ge(sem("w_u"), 16)
                                pool_channels(pe, g + 1).then_inc(sem("u_psum"), 1)
                            if g == 0:
                                pe.wait_ge(sem("w_mix"), 32)
                            pe.wait_ge(sem("pooled"), g + 1)
                            if g >= 2:
                                pe.wait_ge(sem("mixed"), 2 * (g - 1))
                            for h in range(2):
                                m = pe.matmul(banks[4 * (g % 2) + 2 + h][:, :], w_mix[:, g, :], pooled[g % 2][:, h * BANK:(h + 1) * BANK],
                                              start=True, stop=True)
                            m.then_inc(sem("mix_psum"), 1)

                    @block.scalar
                    def _(act):
                        def scaled(g):
                            act.wait_ge(sem("mix_psum"), g + 1)
                            if g == 0:
                                act.wait_ge(sem("w_mix"), 32)
                            for h in range(2):
                                act.activation(mixedT[:, g, h * BANK:(h + 1) * BANK], banks[4 * (g % 2) + 2 + h][:, :], ACT.Copy,
                                               scale=scale_c[:, g:g + 1]).then_inc(sem("mixed"), 1)
                        for g in range(G):
                            if g:
                                act.wait_ge(sem("u_psum"), g)
                                act.wait_ge(sem("pooled"), g)
                            for h in range(2):
                                act.activation(uT[:, PAD + h * BANK:PAD + (h + 1) * BANK], banks[4 * (g % 2) + h][:, :],
                                               ACT.Copy).then_inc(sem("u_kept"), 1)
                            if g:
                                scaled(g - 1)
                        scaled(G - 1)

                    @block.vector
                    def _(dve):
                        dve.wait_ge(sem("consts"), 3 + PAD)
                        step = 0
                        for g, window in enumerate(POOL_WINDOWS):
                            dve.wait_ge(sem("u_kept"), 2 * g + 2)
                            if g >= 2:
                                dve.wait_ge(sem("mix_psum"), g - 1)
                            src, shift = uT, 1
                            while shift < window:
                                dst = sums[(shift.bit_length() - 1) % 2]
                                dve.tensor_tensor(dst[:, PAD:PAD + S], src[:, PAD:PAD + S], src[:, PAD - shift:PAD + S - shift],
                                                  ALU.add).then_inc(sem("sum"), 1)
                                step += 1
                                dve.wait_ge(sem("sum"), step)
                                src, shift = dst, shift * 2
                            dve.tensor_tensor(pooled[g % 2][:, 0:window], src[:, PAD:PAD + window], inv_n[:, 0:window],
                                              ALU.mult).then_inc(sem("sum"), 1)
                            step += 1
                            dve.scalar_tensor_tensor(pooled[g % 2][:, window:S], src[:, PAD + window:PAD + S], 1.0 / window,
                                                     uT[:, PAD + window:PAD + S], ALU.mult, ALU.subtract)
                            dve.wait_ge(sem("sum"), step)
                            dve.tensor_tensor(pooled[g % 2][:, 0:window], pooled[g % 2][:, 0:window], uT[:, PAD:PAD + window],
                                              ALU.subtract).then_inc(sem("pooled"), 1)

        def attend():
            ctx, sem = stage("att")
            with ctx:
                qTh = [view(arena_m, 1024 * b, S) for b in (0, 1)]
                kTh = [view(arena_m, 2048 + 1024 * b, S) for b in (0, 1)]
                prob = [view(arena_m, 4096 + 1024 * b, S) for b in (0, 1)]
                probT = [view(arena_m, 6144 + 1024 * b, T, P) for b in (0, 1)]
                head_words = T * (2 * HD + V)
                qst = [view(arena_w, spare_w + head_words * b, T, HD) for b in (0, 1)]
                kst = [view(arena_w, spare_w + head_words * b + T * HD, T, HD) for b in (0, 1)]
                vst = [view(arena_w, spare_w + head_words * b + 2 * T * HD, T, V) for b in (0, 1)]
                base = spare_w + 2 * head_words
                negmax = [view(arena_w, base + b, 1) for b in (0, 1)]
                total = [view(arena_w, base + 2 + b, 1) for b in (0, 1)]
                rtotal = [view(arena_w, base + 4 + b, 1) for b in (0, 1)]
                maskb = sb("a_mask", [P, P], BF16, ctx=ctx)
                identb = sb("a_ident", [P, P], BF16, ctx=ctx)
                SCALE = float(1.0 / np.sqrt(HD))
                score = [banks[0:2], banks[2:4]]
                turn = banks[4:6]
                obank = banks[6:8]
                AHEAD = 2

                with nc.Block() as block:
                    @block.gpsimd
                    def _(pool):
                        pool.memset(maskb[:, :], 0.0).then_inc(sem("c"), 1)
                        pool.wait_ge(sem("c"), 1)
                        pool.affine_select(out=maskb[:, :], in_=maskb[:, :], compare_op=ALU.is_ge, fill=NEG, base=0,
                                           pattern=[[-1, P]], channel_multiplier=1).then_inc(sem("consts"), 1)
                        pool.tensor_copy(identb[:, :], ident[:, :]).then_inc(sem("consts"), 1)

                        def fetch(h, b):
                            if not isinstance(h, int):
                                wait_value(pool, sem("o_psum"), 2 * h - 2)
                            pool.tensor_copy(qst[b], q_full[:, :, bass.ds(h, 1), :].rearrange("p t o d -> p t (o d)"))
                            pool.tensor_copy(kst[b], k_full[:, :, bass.ds(h, 1), :].rearrange("p t o d -> p t (o d)"))
                            pool.tensor_copy(vst[b], v_full[:, :, bass.ds(h, 1), :].rearrange("p t o d -> p t (o d)")
                                             ).then_inc(sem("fetched"), 1)
                        pool.tensor_copy(vst[0], v_full[:, :, 0, :]).then_inc(sem("fetched"), 1)
                        fetch(1, 1)
                        pair_loop(pool, H, fetch, first=2)

                    def fills(h, b):
                        return [(src, dst[b], half) for src, dst in ((qst[b], qTh), (kst[b], kTh)) for half in (0, 1)]

                    def is_first(h):
                        return isinstance(h, int) and h == 0

                    def head_loop(eng, start, body):
                        start()
                        body(0, 0, True, 0)
                        with eng.Fori(0, HP - 1) as i:
                            body(2 * i + 1, 1, True, i)
                            body(2 * i + 2, 0, True, i + 1)
                        body(H - 1, 1, False, HP - 1)

                    @block.tensor
                    def _(pe):
                        def turn_head(h, b):
                            if is_first(h):
                                pe.wait_ge(sem("fetched_0"), 2)
                            wait_value(pe, sem("fetched"), h + 1)
                            for j, (src, dst, half) in enumerate(fills(h, b)):
                                if j >= 2:
                                    wait_value(pe, sem("qk_kept"), 4 * h + (j - 1))
                                for t in range(4):
                                    m = pe.transpose(turn[half][0:HD, t * P:(t + 1) * P], src[:, 4 * half + t, :], ident[:, :])
                                m.then_inc(sem("qk_psum"), 1)

                        def scores(h, b, s):
                            if s == 0:
                                wait_value(pe, sem("qk_kept"), 4 * h + 4)
                            if not (is_first(h) and s < AHEAD):
                                wait_value(pe, sem("exps"), T * h + (s - 1))
                            width = (s + 1) * P
                            for j in range(0, width, BANK):
                                w = min(BANK, width - j)
                                last = j + w == width
                                m = pe.matmul(score[s % 2][j // BANK][:, 0:w], qTh[b][0:HD, s * P:(s + 1) * P], kTh[b][0:HD, j:j + w],
                                              start=True, stop=not last, skip_group_check=True)
                            m = pe.matmul(score[s % 2][s // 4][:, w - P:w], identb[:, :], maskb[:, :], start=False, stop=True,
                                          skip_group_check=True)
                            m.then_inc(sem("scores"), 1)

                        def kept(h, s):
                            return T * 3 // 2 * h + sum(1 + (j > 3) for j in range(s + 1))

                        def values(h, b, s):
                            wait_value(pe, sem("probT_kept"), kept(h, s))
                            for t in range(s + 1):
                                m = pe.matmul(obank[s // 4][b * V:(b + 1) * V, (s % 4) * P:(s % 4 + 1) * P], vst[b][:, t, :],
                                              probT[s % 2][:, t, :], start=(t == 0), stop=(t == s))
                            if s % 4 == 3:
                                m.then_inc(sem("o_psum"), 1)

                        def step(h, b, s, more):
                            if s + AHEAD < T:
                                scores(h, b, s + AHEAD)
                            elif more:
                                scores(h + 1, 1 - b, s + AHEAD - T)
                            if s == 4 and more:
                                wait_value(pe, sem("qk_kept"), 4 * h + 8)
                            wait_value(pe, sem("normed"), T * h + (s + 1))
                            if s:
                                wait_value(pe, sem("probT_kept"), kept(h, s - 1))
                            elif not is_first(h):
                                wait_value(pe, sem("probT_kept"), kept(h - 1, T - 1))
                            for t in range(s + 1):
                                m = pe.transpose(turn[t // 4][:, (t % 4) * P:(t % 4 + 1) * P], prob[s % 2][:, t * P:(t + 1) * P], ident[:, :])
                                if t in (3, s):
                                    m.then_inc(sem("probT_psum"), 1)
                            if s:
                                values(h, b, s - 1)
                            elif not is_first(h):
                                values(h - 1, 1 - b, T - 1)
                            if s == 3 and more:
                                wait_value(pe, sem("probT_kept"), kept(h, 3))
                                turn_head(h + 1, 1 - b)
                            if s == T - 1 and not more:
                                values(h, b, s)

                        def start():
                            pe.wait_ge(sem("consts"), 2)
                            turn_head(0, 0)
                            scores(0, 0, 0)
                            scores(0, 0, 1)

                        def body(h, b, more, pair):
                            for s in range(T):
                                step(h, b, s, more)
                        head_loop(pe, start, body)

                    @block.scalar
                    def _(act):
                        def keep_q(h, b):
                            for j, (src, dst, half) in enumerate(fills(h, b)):
                                wait_value(act, sem("qk_psum"), 4 * h + (j + 1))
                                act.activation(dst[0:HD, half * BANK:(half + 1) * BANK], turn[half][0:HD, :], ACT.Copy).then_inc(sem("qk_kept"), 1)

                        def exps(h, s):
                            wait_value(act, sem("maxes"), T * h + (s + 1))
                            n1 = min(s + 1, 4) * P
                            two = s >= 4
                            pair = score[s % 2]
                            if two:
                                act.activation(prob[s % 2][:, 0:BANK], pair[0][:, :], ACT.Exp, bias=negmax[s % 2], scale=SCALE,
                                               accum_out=total[s % 2])
                                act.activation(prob[s % 2][:, BANK:(s + 1) * P], pair[1][:, 0:(s - 3) * P], ACT.Exp, bias=negmax[s % 2],
                                               scale=SCALE, accum_out=total2[s % 2]).then_inc(sem("exps"), 1)
                            else:
                                act.activation(prob[s % 2][:, 0:n1], pair[0][:, 0:n1], ACT.Exp, bias=negmax[s % 2], scale=SCALE,
                                               accum_out=total[s % 2]).then_inc(sem("exps"), 1)

                        total2 = [view(arena_w, base + 6 + b, 1) for b in (0, 1)]

                        def step(h, b, s, more, pair):
                            wait_value(act, sem("probT_psum"), 12 * h + sum(1 + (j > 3) for j in range(s + 1)))
                            if s + AHEAD < T:
                                exps(h, s + AHEAD)
                            elif more:
                                exps(h + 1, s + AHEAD - T)
                            if s >= 4:
                                act.activation(probT[s % 2][:, 4:s + 1, :].rearrange("p t q -> p (t q)"), turn[1][:, 0:(s - 3) * P],
                                               ACT.Copy).then_inc(sem("probT_kept"), 1)
                            if s == 3 and more:
                                keep_q(h + 1, 1 - b)
                            if s == 4:
                                keep_out(h, b, pair, 0)
                            if s == 0 and not is_first(h):
                                keep_out(h - 1, 1 - b, pair if b else pair - 1, 1)

                        def keep_out(h, b, pair, half):
                            wait_value(act, sem("o_psum"), 2 * h + (half + 1))
                            rows = attnT[b * V:(b + 1) * V, bass.ds(pair, 1), :].rearrange("p o s -> p (o s)")
                            act.activation(rows[:, half * BANK:(half + 1) * BANK], obank[half][b * V:(b + 1) * V, :],
                                           ACT.Copy)

                        def start():
                            act.activation(kst[0], k_full[:, :, 0, :], ACT.Copy).then_inc(sem("fetched_0"), 1)
                            keep_q(0, 0)
                            exps(0, 0)
                            exps(0, 1)

                        def body(h, b, more, pair):
                            for s in range(T):
                                step(h, b, s, more, pair)
                            if not more:
                                keep_out(h, b, pair, 1)
                        head_loop(act, start, body)

                    @block.vector
                    def _(dve):
                        mpair = [view(arena_w, base + 8 + 2 * b, 2) for b in (0, 1)]
                        total2 = [view(arena_w, base + 6 + b, 1) for b in (0, 1)]
                        tsum = [view(arena_w, base + 12 + b, 1) for b in (0, 1)]

                        def maxes(h, s):
                            wait_value(dve, sem("scores"), T * h + (s + 1))
                            pair = score[s % 2]
                            r = dve.tensor_reduce(mpair[s % 2][:, 0:1], pair[0][:, 0:min(s + 1, 4) * P], AX.X, ALU.max)
                            if s >= 4:
                                r = dve.tensor_reduce(mpair[s % 2][:, 1:2], pair[1][:, 0:(s - 3) * P], AX.X, ALU.max)
                            r.then_inc(sem("m"), 1)
                            wait_value(dve, sem("m"), T * h + (s + 1))
                            if s >= 4:
                                dve.tensor_scalar(negmax[s % 2], mpair[s % 2][:, 0:1], mpair[s % 2][:, 1:2], -SCALE, ALU.max,
                                                  ALU.mult).then_inc(sem("maxes"), 1)
                            else:
                                dve.tensor_scalar(negmax[s % 2], mpair[s % 2][:, 0:1], -SCALE, None, ALU.mult).then_inc(sem("maxes"), 1)

                        def step(h, b, s, more):
                            wait_value(dve, sem("exps"), T * h + (s + 1))
                            if s >= 4:
                                dve.tensor_tensor(tsum[s % 2], total[s % 2], total2[s % 2], ALU.add).then_inc(sem("d"), 1)
                                wait_value(dve, sem("d"), 4 * h + (s - 3))
                                dve.reciprocal(rtotal[s % 2], tsum[s % 2]).then_inc(sem("r"), 1)
                            else:
                                dve.reciprocal(rtotal[s % 2], total[s % 2]).then_inc(sem("r"), 1)
                            wait_value(dve, sem("r"), T * h + (s + 1))
                            dve.tensor_scalar(prob[s % 2][:, 0:(s + 1) * P], prob[s % 2][:, 0:(s + 1) * P], rtotal[s % 2], None,
                                              ALU.mult).then_inc(sem("normed"), 1)
                            if s + AHEAD < T:
                                maxes(h, s + AHEAD)
                            elif more:
                                maxes(h + 1, s + AHEAD - T)
                            wait_value(dve, sem("probT_psum"), 12 * h + (sum(1 + (j > 3) for j in range(s)) + 1))
                            n = min(s + 1, 4)
                            dve.tensor_copy(probT[s % 2][:, 0:n, :].rearrange("p t q -> p (t q)"), turn[0][:, 0:n * P]).then_inc(sem("probT_kept"), 1)

                        def start():
                            dve.tensor_copy(qst[0], q_full[:, :, 0, :]).then_inc(sem("fetched_0"), 1)
                            maxes(0, 0)
                            maxes(0, 1)

                        def body(h, b, more, pair):
                            for s in range(T):
                                step(h, b, s, more)
                        head_loop(dve, start, body)

        def merge():
            ctx, sem = stage("merge")
            with ctx:
                WB = 8192
                wga = [view(arena_w, WB + 3072 * b, K, P) for b in (0, 1)]
                wgp = [view(arena_w, WB + 3072 * b + 1024, K, P) for b in (0, 1)]
                wya = [view(arena_w, WB + 3072 * b + 2048, KA, P) for b in (0, 1)]
                wyp = [view(arena_w, WB + 3072 * b + 2560, KO, P) for b in (0, 1)]
                sig = [[view(arena_w, WB + 6144 + 512 * (2 * n + j), BANK) for j in (0, 1)] for n in (0, 1)]
                prod = [[view(arena_w, WB + 8192 + 512 * (2 * n + j), BANK) for j in (0, 1)] for n in (0, 1)]
                with nc.Block() as block:
                    @block.sync
                    def _(sp):
                        def columns(lo, c):
                            if isinstance(c, int):
                                return slice(lo + c * P, lo + (c + 1) * P)
                            return bass.ds(c * P + lo, P)

                        def load(c, b):
                            s = sem(f"w{b}")
                            sp.dma_start(wga[b], w_in[:, columns(GATE_A, c)].rearrange("(k p) n -> p k n", p=P)).then_inc(s, 16)
                            sp.dma_start(wgp[b], w_in[:, columns(GATE_P, c)].rearrange("(k p) n -> p k n", p=P)).then_inc(s, 16)
                            sp.dma_start(wya[b], w_attn_out[:, columns(0, c)].rearrange("(k p) n -> p k n", p=P)).then_inc(s, 16)
                            sp.dma_start(wyp[b], w_pool_out[:, columns(0, c)].rearrange("(k p) n -> p k n", p=P)).then_inc(s, 16)
                        load(0, 0)
                        load(1, 1)
                        sp.dma_start(view(arena_w, 0, K, D), w_o.rearrange("(k p) n -> p k n", p=P)).then_inc(sem("w_o"), 16)
                        with sp.Fori(1, K // 2) as i:
                            for b in (0, 1):
                                wait_value(sp, sem("psum_full"), 4 * i + (2 * b - 2))
                                load(2 * i + b, b)
                        sp.wait_ge(sem("w_o"), 16)

                    @block.tensor
                    def _(pe):
                        def column(c, b):
                            wait_value(pe, sem(f"w{b}"), 32 * c + (64 - 32 * b))
                            for n in (0, 1):
                                ga, gp, ya, yp = banks[4 * n:4 * n + 4]
                                half = slice(n * BANK, (n + 1) * BANK)
                                if not (isinstance(c, int) and c == 0):
                                    wait_value(pe, sem("psum_read"), 2 * c + (n - 1))
                                for bank, w, src, kk in ((ga, wga, hT, K), (gp, wgp, hT, K), (ya, wya, attnT, KA), (yp, wyp, mixedT, KO)):
                                    for k in range(kk):
                                        m = pe.matmul(bank[:, :], w[b][:, k, :], src[:, k, half], start=(k == 0), stop=(k == kk - 1))
                                    if bank is gp:
                                        m.then_inc(sem("gates_psum"), 1)
                                m.then_inc(sem("psum_full"), 1)
                        column(0, 0)
                        with pe.Fori(0, K // 2 - 1) as i:
                            column(2 * i + 1, 1)
                            column(2 * i + 2, 0)
                        column(K - 1, 1)

                    @block.scalar
                    def _(act):
                        def column(c, b):
                            for n in (0, 1):
                                wait_value(act, sem("gates_psum"), 2 * c + (n + 1))
                                if not (isinstance(c, int) and c == 0):
                                    wait_value(act, sem("psum_read"), 2 * c + (n - 1))
                                for j in (0, 1):
                                    act.activation(sig[n][j], banks[4 * n + j][:, :], ACT.Sigmoid).then_inc(sem("sig"), 1)
                        column(0, 0)
                        with act.Fori(0, K // 2 - 1) as i:
                            column(2 * i + 1, 1)
                            column(2 * i + 2, 0)
                        column(K - 1, 1)

                    @block.vector
                    def _(dve):
                        def column(c, b):
                            for n in (0, 1):
                                wait_value(dve, sem("psum_full"), 2 * c + (n + 1))
                                wait_value(dve, sem("sig"), 4 * c + (2 * n + 2))
                                if not (isinstance(c, int) and c == 0):
                                    wait_value(dve, sem("merged"), 2 * c + (n - 1))
                                dve.tensor_tensor(prod[n][0], banks[4 * n + 2][:, :], sig[n][0], ALU.mult)
                                dve.tensor_tensor(prod[n][1], banks[4 * n + 3][:, :], sig[n][1], ALU.mult).then_inc(sem("psum_read"), 1)
                        column(0, 0)
                        with dve.Fori(0, K // 2 - 1) as i:
                            column(2 * i + 1, 1)
                            column(2 * i + 2, 0)
                        column(K - 1, 1)

                    @block.gpsimd
                    def _(pool):
                        def column(c, b):
                            for n in (0, 1):
                                wait_value(pool, sem("psum_read"), 2 * c + (n + 1))
                                pool.tensor_tensor(mT[:, bass.ds(c, 1), n * BANK:(n + 1) * BANK].rearrange("p o s -> p (o s)"),
                                                   prod[n][0], prod[n][1], ALU.add).then_inc(sem("merged"), 1)
                        pair_loop(pool, K, column)

        def route():
            ctx, sem = stage("route")
            with ctx:
                w_out = view(arena_w, 0, K, D)
                xt = [view(arena_a, D * b, D) for b in (0, 1)]
                x1 = [view(arena_a, D * (2 + b), D) for b in (0, 1)]
                h2 = [view(arena_a, D * (4 + b), D) for b in (0, 1)]
                junk = view(arena_a, D * 6, D)
                mts = [view(arena_h, D * b, K, P) for b in (0, 1)]
                h2T = [view(arena_h, D * (2 + b), K, P) for b in (0, 1)]
                w_r = view(arena_h, 4096, K, E)
                b_r = view(arena_h, 4352, E)
                zeros = view(arena_h, 4608, SLOTS // P).bitcast(I32)
                tok = view(arena_h, 5120, T).bitcast(I32)
                part = view(arena_h, 5130, 1)
                ms, rms, rstd = (view(arena_h, 5132 + j, 1) for j in range(3))
                logit = view(arena_h, 5152, E)
                top8 = view(arena_h, 5184, 8)
                idx8 = view(arena_h, 5192, 8).bitcast(U32)
                idxf = view(arena_h, 5200, TOP_K)
                onehot = view(arena_h, 5248, TOP_K, E)
                taken = view(arena_h, 5376, TOP_K, E)
                slot_e = view(arena_h, 5504, E)
                base = view(arena_h, 5536, E)
                destf = view(arena_h, 5568, TOP_K)
                dst = [view(arena_h, 5576 + 4 * b, TOP_K).bitcast(I32) for b in (0, 1)]
                tokb = [view(arena_h, 5584 + b, 1).bitcast(I32) for b in (0, 1)]
                top_all = view(arena_h, 5632, T, 8)
                expo = view(arena_h, 5696, T, TOP_K)
                esum, ersum = view(arena_h, 5728, T), view(arena_h, 5736, T)
                c_0, c_a, c_b = (view(arena_h, 5760 + 2 * E * j, 2, E) for j in range(3))
                nit, cnt = c_0[:, 0, :], c_0[:, 1, :]
                eid, before, chunk, count, lo, cap, row = (view(arena_h, 6000 + j, 1) for j in range(7))
                le, tmp, oh, first, shift_e = (view(arena_a, 7424 + E * j, E) for j in range(5))
                slot_all, e_all, row_all = (view(arena_a, 7168 + T * TOP_K * j, T, TOP_K) for j in range(3))
                oh_all = view(arena_h, 6144, T * TOP_K, E)
                fields = view(arena_h, 6016, ITEM_FIELDS)
                fields_i = view(arena_h, 6024, ITEM_FIELDS).bitcast(I32)
                start_e = view(arena_h, 6048, E)
                earlier = sb("r_earlier", [P, P], BF16, ctx=ctx)
                ones = sb("r_ones", [P, P], BF16, ctx=ctx)
                chosen = sb("r_chosen", [P, E], BF16, ctx=ctx)
                TB0, TB1, LG, RK = banks[4:8]
                with nc.Block() as block:
                    @block.sync
                    def _(sp):
                        sp.dma_start(gain_row[:, :], g_ffn[0].partition_broadcast(P)).then_inc(sem("gain"), 16)
                        for b in (0, 1):
                            sp.dma_start(xt[b], x2d[b * P:(b + 1) * P, :]).then_inc(sem(f"x{b}"), 16)
                        sp.dma_start(w_r, w_router[0].rearrange("(k p) n -> p k n", p=P)).then_inc(sem("w_r"), 16)
                        sp.dma_start(b_r, b_router[0].partition_broadcast(P)).then_inc(sem("w_r"), 16)
                        sp.wait_ge(sem("zeros"), 1)
                        sp.dma_start(list_dram.rearrange("(p s) o -> p (s o)", p=P), zeros).then_inc(sem("listed"), 16)

                        def store(n, b):
                            wait_value(sp, sem("h2_ready"), n + 1)
                            sp.dma_start(x1_dram[bass.ds(n * P, P), :], x1[b]).then_inc(sem("stored"), 16)
                            sp.dma_start(h2_dram[bass.ds(n * P, P), :], h2[b]).then_inc(sem("stored"), 16)
                            wait_value(sp, sem("stored"), 32 * n + 32)
                            sp.sem_inc(sem("rows_free"), 1)

                        sp.sem_inc(sem("rows_free"), 2)
                        with sp.Fori(0, T // 2 - 1) as i:
                            for b in (0, 1):
                                wait_value(sp, sem("x1_sum"), 2 * i + (b + 1))
                                sp.dma_start(xt[b], x2d[bass.ds(i * (2 * P) + (2 + b) * P, P), :]).then_inc(sem(f"x{b}"), 16)
                                store(2 * i + b, b)
                        store(T - 2, 0)
                        store(T - 1, 1)
                        sp.wait_ge(sem("fields"), 1)
                        sp.dma_start(item_dram, fields_i[0:ITEM_ROWS, :]).then_inc(sem("table"), 16)
                        sp.wait_ge(sem("table"), 16)
                        sp.dma_start(items[:, :], item_dram.rearrange("(o i) f -> o (i f)", o=1)).then_inc(sem("table"), 16)
                        sp.wait_ge(sem("table"), 32)

                    @block.gpsimd
                    def _(pool):
                        pool.memset(zeros, 0).then_inc(sem("zeros"), 1)
                        pool.iota(tok, pattern=[[P, T]], base=0, channel_multiplier=1).then_inc(sem("consts"), 1)
                        pool.iota(part, pattern=[[1, 1]], base=0, channel_multiplier=1,
                                  allow_small_or_imprecise_dtypes=True).then_inc(sem("consts"), 1)
                        pool.memset(ones[:, :], 1.0).then_inc(sem("consts"), 1)
                        pool.memset(earlier[:, :], 1.0).then_inc(sem("pc"), 1)
                        pool.wait_ge(sem("pc"), 1)
                        pool.affine_select(out=earlier[:, :], in_=earlier[:, :], compare_op=ALU.is_gt, fill=0.0, base=0,
                                           pattern=[[1, P]], channel_multiplier=-1).then_inc(sem("consts"), 1)

                        def fetch(n, b):
                            if not isinstance(n, int):
                                wait_value(pool, sem("x1_psum"), n - 1)
                            pool.tensor_copy(mts[b], mT[:, :, bass.ds(n * P, P)]).then_inc(sem("fetched"), 1)

                        def scatter(n, b):
                            pool.tensor_copy(tokb[b], tok[:, bass.ds(n, 1)]).then_inc(sem("tokb"), 1)
                            wait_value(pool, sem("dst"), n + 1)
                            wait_value(pool, sem("tokb"), n + 1)
                            for j in range(TOP_K):
                                pool.indirect_dma_start(list_dram, bass.IndirectOffsetOnAxis(dst[b][:, j:j + 1], 0), tokb[b], None
                                                        ).then_inc(sem("scattered"), 16)
                            wait_value(pool, sem("scattered"), 64 * n + 64)
                            pool.sem_inc(sem("dst_free"), 1)
                        pool.sem_inc(sem("dst_free"), 2)
                        fetch(1, 1)
                        pool.wait_ge(sem("listed"), 16)
                        pool.wait_ge(sem("consts"), 4)
                        with pool.Fori(0, T // 2 - 1) as i:
                            for b in (0, 1):
                                fetch(2 * i + (2 + b), b)
                                scatter(2 * i + b, b)
                        scatter(T - 2, 0)
                        scatter(T - 1, 1)
                        pool.wait_ge(sem("stored"), 32 * T)
                        gather_rows(pool, 0, 0)

                    @block.tensor
                    def _(pe):
                        def project(n, b, between):
                            if isinstance(n, int) and n == 0:
                                tile = mT[:, :, 0:P]
                            else:
                                wait_value(pe, sem("fetched"), n)
                                tile = mts[b]
                            for part in range(4):
                                j = part // 2
                                for k in range(part % 2 * K // 2, (part % 2 + 1) * K // 2):
                                    m = pe.matmul(banks[2 * b + j][:, :], tile[:, k, :], w_out[:, k, j * BANK:(j + 1) * BANK],
                                                  start=(k == 0), stop=(k == K - 1))
                                if part == 3:
                                    m.then_inc(sem("x1_psum"), 1)
                                if between and part:
                                    between[part - 1](n - 1, 1 - b)

                        def turn(n, b):
                            wait_value(pe, sem("h2_ready"), n + 1)
                            for k in range(K):
                                m = pe.transpose((TB0, TB1)[k // 4][:, (k % 4) * P:(k % 4 + 1) * P], h2[b][:, k * P:(k + 1) * P], ident[:, :])
                            m.then_inc(sem("h2T_psum"), 1)

                        def logits(n, b):
                            wait_value(pe, sem("h2T"), 2 * n + 2)
                            for k in range(K):
                                m = pe.matmul(LG[:, 0:E], h2T[b][:, k, :], w_r[:, k, :], start=(k == 0), stop=(k == K - 1))
                            m.then_inc(sem("logits"), 1)

                        def ranks(n, b):
                            wait_value(pe, sem("chosen"), n + 1)
                            pe.matmul(RK[:, 0:E], earlier[:, :], chosen[:, :], start=True, stop=True)
                            pe.matmul(RK[:, E:2 * E], ones[:, :], chosen[:, :], start=True, stop=True).then_inc(sem("ranks"), 1)

                        project(0, 0, None)
                        pe.wait_ge(sem("w_r"), 32)
                        pe.wait_ge(sem("consts"), 4)
                        with pe.Fori(0, T // 2 - 1) as i:
                            for b in (0, 1):
                                project(2 * i + (b + 1), 1 - b, (turn, logits, ranks))
                        project(T - 1, 1, (turn, logits, ranks))
                        for router in (turn, logits, ranks):
                            router(T - 1, 1)

                    @block.scalar
                    def _(act):
                        def norm(n, b):
                            wait_value(act, sem("x1_sum"), n + 1)
                            act.activation(junk, x1[b], ACT.Square, scale=float(D) ** -0.5, accum_out=ms).then_inc(sem("ms"), 1)
                            wait_value(act, sem("ms"), n + 1)
                            act.activation(rms, ms, ACT.Sqrt, bias=eps[:, :]).then_inc(sem("rms"), 1)

                        def keep(n, b):
                            wait_value(act, sem("h2T_psum"), n + 1)
                            act.activation(h2T[b][:, 0:4, :].rearrange("p k t -> p (k t)"), TB0[:, :], ACT.Copy).then_inc(sem("h2T"), 1)
                        norm(0, 0)
                        for c in (2, 3):
                            load_gate_up(act, 0, c)
                        for c in range(D // CW):
                            load_down(act, 0, c)
                        with act.Fori(0, T // 2 - 1) as i:
                            for b in (0, 1):
                                keep(2 * i + b, b)
                                norm(2 * i + (b + 1), 1 - b)
                        keep(T - 2, 0)
                        norm(T - 1, 1)
                        for c in (0, 1):
                            load_gate_up(act, 0, c)
                        keep(T - 1, 1)
                        act.wait_ge(sem("shifted"), 1)
                        act.activation(expo, expo, ACT.Exp).then_inc(sem("expo"), 1)

                    @block.vector
                    def _(dve):
                        done = [0]

                        def then(instruction):
                            instruction.then_inc(sem("chain"), 1)
                            done[0] += 1
                            dve.wait_ge(sem("chain"), done[0])

                        dve.wait_ge(sem("w_r"), 32)
                        dve.wait_ge(sem("gain"), 16)
                        then(dve.tensor_scalar(start_e, iota_e[:, :], float(S), None, ALU.mult))
                        then(dve.tensor_copy(base, start_e))

                        def norm(n, b):
                            wait_value(dve, sem("x1_psum"), n + 1)
                            wait_value(dve, sem(f"x{b}"), 8 * n + (16 - 8 * b))
                            wait_value(dve, sem("rows_free"), n + 1)
                            for j in (0, 1):
                                half = slice(j * BANK, (j + 1) * BANK)
                                m = dve.tensor_tensor(x1[b][:, half], banks[2 * b + j][:, :], xt[b][:, half], ALU.add)
                            m.then_inc(sem("x1_sum"), 1)
                            wait_value(dve, sem("rms"), n + 1)
                            dve.reciprocal(rstd, rms).then_inc(sem("rstd"), 1)
                            wait_value(dve, sem("rstd"), n + 1)
                            dve.scalar_tensor_tensor(h2[b], x1[b], rstd, gain_row[:, :], ALU.mult, ALU.mult).then_inc(sem("h2_ready"), 1)

                        def choose(n, b):
                            steps = 7

                            def step(j, instruction):
                                instruction.then_inc(sem("v"), 1)
                                wait_value(dve, sem("v"), steps * n + (j + 1))
                            wait_value(dve, sem("h2T_psum"), n + 1)
                            dve.tensor_copy(h2T[b][:, 4:8, :].rearrange("p k t -> p (k t)"), TB1[:, :]).then_inc(sem("h2T"), 1)
                            wait_value(dve, sem("logits"), n + 1)
                            step(0, dve.tensor_tensor(logit, LG[:, 0:E], b_r, ALU.add))
                            step(1, dve.max(top8, logit))
                            step(2, dve.max_index(idx8, top8, logit))
                            dve.tensor_copy(top_all[:, bass.ds(n, 1), :].rearrange("p o e -> p (o e)"), top8)
                            step(3, dve.tensor_copy(idxf, idx8[:, 0:TOP_K]))
                            step(4, dve.tensor_tensor(onehot, iota_e[:, :].unsqueeze(1).broadcast_to([P, TOP_K, E]),
                                                      idxf.unsqueeze(2).broadcast_to([P, TOP_K, E]), ALU.is_equal))
                            dve.tensor_reduce(chosen[:, :], onehot.rearrange("p k e -> p e k"), AX.X, ALU.max).then_inc(sem("chosen"), 1)
                            wait_value(dve, sem("ranks"), n + 1)
                            step(5, dve.tensor_tensor(slot_e, RK[:, 0:E], base, ALU.add))
                            dve.tensor_tensor(base, RK[:, E:2 * E], base, ALU.add).then_inc(sem("base"), 1)
                            step(6, dve.tensor_tensor(taken, onehot, slot_e.unsqueeze(1).broadcast_to([P, TOP_K, E]), ALU.mult))
                            dve.tensor_reduce(destf, taken, AX.X, ALU.add).then_inc(sem("destf"), 1)
                            wait_value(dve, sem("destf"), n + 1)
                            dve.tensor_copy(slot_all[:, bass.ds(n, 1), :].rearrange("p o k -> p (o k)"), destf)
                            dve.tensor_copy(e_all[:, bass.ds(n, 1), :].rearrange("p o k -> p (o k)"), idxf)
                            wait_value(dve, sem("dst_free"), n + 1)
                            dve.tensor_copy(dst[b], destf).then_inc(sem("dst"), 1)

                        norm(0, 0)
                        with dve.Fori(0, T // 2 - 1) as i:
                            for b in (0, 1):
                                choose(2 * i + b, b)
                                norm(2 * i + (b + 1), 1 - b)
                        choose(T - 2, 0)
                        norm(T - 1, 1)
                        choose(T - 1, 1)

                        dve.wait_ge(sem("base"), T)
                        dve.tensor_tensor(expo, top_all[:, :, 0:TOP_K], top_all[:, :, 0:1].broadcast_to([P, T, TOP_K]),
                                          ALU.subtract).then_inc(sem("shifted"), 1)
                        dve.wait_ge(sem("expo"), 1)
                        then(dve.tensor_reduce(esum, expo, AX.X, ALU.add))
                        then(dve.reciprocal(ersum, esum))
                        then(dve.tensor_tensor(gates_all[:, :, :], expo, ersum.unsqueeze(2).broadcast_to([P, T, TOP_K]), ALU.mult))

                        dve.wait_ge(sem("consts"), 4)
                        then(dve.tensor_tensor(cnt, base, start_e, ALU.subtract))
                        then(dve.tensor_scalar(nit, cnt, 0.0, 1.0, ALU.mult, ALU.add))
                        for j in range(1, (S + WIDTH - 1) // WIDTH):
                            then(dve.scalar_tensor_tensor(nit, cnt, float(j * WIDTH), nit, ALU.is_gt, ALU.add))
                        src, other, shift = c_a, c_b, 1
                        then(dve.tensor_copy(c_a, c_0))
                        while shift < E:
                            dve.tensor_copy(other[:, :, 0:shift], src[:, :, 0:shift])
                            then(dve.tensor_tensor(other[:, :, shift:E], src[:, :, shift:E], src[:, :, 0:E - shift], ALU.add))
                            src, other, shift = other, src, 2 * shift
                        then(dve.tensor_tensor(first, src[:, 1, :], cnt, ALU.subtract))
                        then(dve.tensor_scalar(le, src[:, 0, :], part, None, ALU.is_le))
                        then(dve.tensor_reduce(eid, le, AX.X, ALU.add))
                        then(dve.tensor_scalar(eid, eid, float(E - 1), None, ALU.min))
                        then(dve.tensor_tensor(tmp, le, nit, ALU.mult))
                        then(dve.tensor_reduce(before, tmp, AX.X, ALU.add))
                        then(dve.tensor_tensor(chunk, part, before, ALU.subtract))
                        then(dve.tensor_scalar(oh, iota_e[:, :], eid, None, ALU.is_equal))
                        then(dve.tensor_tensor(tmp, oh, cnt, ALU.mult))
                        then(dve.tensor_reduce(count, tmp, AX.X, ALU.add))
                        then(dve.tensor_tensor(tmp, oh, first, ALU.mult))
                        then(dve.tensor_reduce(row, tmp, AX.X, ALU.add))
                        then(dve.tensor_scalar(cap, count, -float(WIDTH), 0.0, ALU.add, ALU.max))
                        then(dve.tensor_scalar(lo, chunk, float(WIDTH), 0.0, ALU.mult, ALU.max))
                        then(dve.tensor_tensor(lo, lo, cap, ALU.min))
                        dve.tensor_copy(fields[:, 0:1], eid)
                        dve.scalar_tensor_tensor(fields[:, 1:2], eid, float(S), lo, ALU.mult, ALU.add)
                        dve.tensor_scalar(fields[:, 2:3], count, float(WIDTH), None, ALU.min)
                        dve.tensor_tensor(fields[:, 4:5], row, lo, ALU.add)
                        then(dve.tensor_copy(fields[:, 3:4], src[:, 0, E - 1:E]))
                        dve.tensor_copy(fields_i, fields).then_inc(sem("fields"), 1)

                        then(dve.tensor_tensor(shift_e, first, start_e, ALU.subtract))
                        then(dve.tensor_tensor(oh_all, iota_e[:, :].unsqueeze(1).broadcast_to([P, T * TOP_K, E]),
                                               e_all.rearrange("p t k -> p (t k)").unsqueeze(2).broadcast_to([P, T * TOP_K, E]), ALU.is_equal))
                        then(dve.tensor_tensor(oh_all, oh_all, shift_e.unsqueeze(1).broadcast_to([P, T * TOP_K, E]), ALU.mult))
                        then(dve.tensor_reduce(row_all.rearrange("p t k -> p (t k)"), oh_all, AX.X, ALU.add))
                        then(dve.tensor_tensor(row_all, row_all, slot_all, ALU.add))
                        dve.tensor_copy(dest_all[:, :, :], row_all)

        CW = 2 * P
        CH = FF // CW
        wg = [view(arena_w, 2 * K * CW * c, K, CW) for c in range(CH)]
        wu = [view(arena_w, 2 * K * CW * c + K * CW, K, CW) for c in range(CH)]
        wd = [view(arena_w, 2 * K * FF + KF * CW * c, KF, CW) for c in range(D // CW)]
        w_gu_here = [top.enter_context(nc.semaphore(f"w_gu{c}")) for c in range(CH)]
        w_dn_here = [top.enter_context(nc.semaphore(f"w_dn{c}")) for c in range(D // CW)]

        def load_gate_up(eng, e, c):
            for w, at in ((wg, c * CW), (wu, FF + c * CW)):
                eng.dma_start(w[c], w_gate_up[bass.ds(e, 1)][:, :, at:at + CW].rearrange("o (k p) n -> p (o k) n", p=P)).then_inc(w_gu_here[c], 16)

        def load_down(eng, e, c):
            eng.dma_start(wd[c], w_down[bass.ds(e, 1)][:, :, c * CW:(c + 1) * CW].rearrange("o (k p) n -> p (o k) n", p=P)).then_inc(w_dn_here[c], 16)

        REST = WIDTH - P
        xg = view(arena_a, 0, D)
        TURN = 96
        xg2 = view(arena_a, D, D)[0:TURN, :]
        idx_a = view(arena_m, 11 * WIDTH + 32, 1).bitcast(I32)
        idx_b = view(arena_m, 11 * WIDTH + 33, 1).bitcast(I32)[0:REST, :]
        rows_listed, rows_here = (top.enter_context(nc.semaphore(n)) for n in ("rows_listed", "rows_here"))

        def gather_rows(pool, slot, i):
            pool.dma_start(idx_a, list_dram[bass.ds(slot, P), :]).then_inc(rows_listed, 16)
            pool.dma_start(idx_b, list_dram[bass.ds(slot + P, REST), :]).then_inc(rows_listed, 16)
            wait_value(pool, rows_listed, 32 * i + 32)
            pool.indirect_dma_start(xg, None, h2_dram, bass.IndirectOffsetOnAxis(idx_a, 0)).then_inc(rows_here, 16)
            pool.indirect_dma_start(xg2[0:REST, :], None, h2_dram, bass.IndirectOffsetOnAxis(idx_b, 0)).then_inc(rows_here, 16)
            wait_value(pool, rows_here, 32 * i + 32)

        def experts():
            ctx, sem = stage("ex")
            with ctx:
                y_a = view(arena_a, 2 * D, D)
                y_b = view(arena_a, 3 * D, D)[0:REST, :]
                xT = view(arena_a, 4 * D, K, WIDTH)
                actT = view(arena_a, 4 * D + K * WIDTH, KF, WIDTH)
                gc, sg, gs, yT = ([view(arena_m, WIDTH * (2 * j + b), WIDTH) for b in (0, 1)] for j in range(4))
                uc = [view(arena_m, WIDTH * (8 + j), WIDTH) for j in range(3)]
                bias = view(arena_m, 11 * WIDTH, 3 * K)
                GU, TX, DN, YA, YB = banks[0:3], banks[3], banks[4:6], banks[6], banks[7]
                fill_bank = (DN[0], TX, DN[1], GU[2])

                def field(eng, i, f, lo, hi):
                    where = i * ITEM_FIELDS + f
                    return eng.value_load(items[0:1, bass.ds(where, 1)], min_val=lo, max_val=hi)

                def n_items(eng):
                    return field(eng, 0, 3, E, E + S * TOP_K // WIDTH)

                with nc.Block() as block:
                    @block.sync
                    def _(sp):
                        def load(i):
                            e = field(sp, i, 0, 0, E - 1)
                            for c in range(CH):
                                wait_value(sp, sem("gu_psum"), KF * i + (2 * c + 2 - KF))
                                load_gate_up(sp, e, c)
                            for c in range(D // CW):
                                wait_value(sp, sem("dn_psum"), K * i + (2 * c + 2 - K))
                                load_down(sp, e, c)
                        sp.wait_ge(rows_here, 32)
                        sp.dma_start(view(arena_h, 0, K, D), w_ple_gate.rearrange("(k p) n -> p k n", p=P)).then_inc(sem("ple"), 16)
                        sp.dma_start(view(arena_m, 4096, KP, D), w_ple.rearrange("(k p) n -> p k n", p=P)).then_inc(sem("ple"), 16)
                        sp.dma_start(gain_row[:, :], g_ple[0].partition_broadcast(P)).then_inc(sem("ple"), 16)
                        with sp.Fori(1, n_items(sp)) as i:
                            load(i)
                        sp.wait_ge(sem("ple"), 48)

                    @block.gpsimd
                    def _(pool):
                        n = n_items(pool)
                        with pool.Fori(0, n) as i:
                            wait_value(pool, sem("x_psum"), 4 * i + 4)
                            gather_rows(pool, field(pool, i + 1, 1, 0, SLOTS - WIDTH), i + 1)

                    @block.tensor
                    def _(pe):
                        def turn_rows(i, rest):
                            wait_value(pe, rows_here, 32 * i + 32)
                            for j, bank in enumerate(fill_bank):
                                if j == 3 and not isinstance(i, int):
                                    wait_value(pe, sem("gu_read"), KF * i - 2)
                                for h in (0, 1):
                                    d = 2 * j + h
                                    if rest:
                                        pe.transpose(bank[:, h * WIDTH + P:h * WIDTH + P + TURN], xg2[:, d * P:(d + 1) * P],
                                                     ident[0:TURN, 0:TURN])
                                    m = pe.transpose(bank[:, h * WIDTH:h * WIDTH + P], xg[:, d * P:(d + 1) * P], ident[:, :])
                                m.then_inc(sem("x_psum"), 1)

                        def turn_x(i):
                            with pe.If_lt(width_ahead, P + 1):
                                turn_rows(i, False)
                            with pe.Else():
                                turn_rows(i, True)

                        def gate_up(i, width, last_row_tile):
                            wait_value(pe, sem("xT_act"), 2 * i + 2)
                            wait_value(pe, sem("xT_dve"), 2 * i + 2)
                            for f in range(KF):
                                c, at = f // 2, (f % 2) * P
                                if f % 2 == 0:
                                    wait_value(pe, w_gu_here[c], 32 * i + 32)
                                if f >= 3:
                                    wait_value(pe, sem("gu_read"), KF * i + (f - 2))
                                for w, to in ((wg, 0), (wu, WIDTH)):
                                    for k in range(K):
                                        m = pe.matmul(GU[f % 3][:, to:to + width], w[c][:, k, at:at + P], xT[:, k, 0:width],
                                                      start=(k == 0), stop=(k == K - 1), skip_group_check=True)
                                m.then_inc(sem("gu_psum"), 1)
                                if f == 0 and last_row_tile:
                                    turn_y(i - 1, K - 1, True)

                        def down(i, width):
                            for d in range(K):
                                c, at = d // 2, (d % 2) * P
                                if d % 2 == 0:
                                    wait_value(pe, w_dn_here[c], 16 * i + 16)
                                if d < 2:
                                    wait_value(pe, sem("xT_act"), 2 * i + (3 + d))
                                else:
                                    wait_value(pe, sem("yT"), K * i + (d - 1))
                                for k in range(KF):
                                    if d == 0:
                                        wait_value(pe, sem("act"), KF * i + (k + 1))
                                    m = pe.matmul(DN[d % 2][:, 0:width], wd[c][:, k, at:at + P], actT[:, k, 0:width],
                                                  start=(k == 0), stop=(k == KF - 1))
                                m.then_inc(sem("dn_psum"), 1)
                                if d:
                                    turn_y(i, d - 1, width > P)

                        def turn_y(i, d, rest):
                            wait_value(pe, sem("yT"), K * i + (d + 1))
                            if d == 4:
                                wait_value(pe, sem("y_kept"), 4 * i + 2)
                            at = slice((d % 4) * P, (d % 4 + 1) * P)
                            m = pe.transpose(YA[:, at], yT[d % 2][:, 0:P], ident[:, :])
                            if rest:
                                m = pe.transpose(YB[0:REST, at], yT[d % 2][:, P:WIDTH], ident[:, :])
                            m.then_inc(sem("y_psum"), 1)

                        def by_width(tokens, part, widths=WIDTHS):
                            if len(widths) == 1:
                                part(widths[0])
                                return
                            with pe.If_lt(tokens, widths[0] + 1):
                                part(widths[0])
                            with pe.Else():
                                by_width(tokens, part, widths[1:])

                        n = n_items(pe)
                        width_now, width_ahead = pe.alloc_register("width_now"), pe.alloc_register("width_ahead")
                        pe.reg_mov(width_ahead, field(pe, 0, 2, 0, WIDTH))
                        pe.wait_ge(sem("psum_set"), 5)
                        turn_x(0)
                        pe.wait_ge(sem("psum_set"), 8)
                        pe.reg_mov(width_now, width_ahead)
                        by_width(width_now, lambda width: gate_up(0, width, False))
                        with pe.Fori(0, n) as i:
                            pe.reg_mov(width_ahead, field(pe, i + 1, 2, 0, WIDTH))
                            turn_x(i + 1)
                            by_width(width_now, lambda width: down(i, width))
                            pe.reg_mov(width_now, width_ahead)
                            with pe.If(i + 1 < n):
                                by_width(width_now, lambda width: gate_up(i + 1, width, True))
                            with pe.Else():
                                turn_y(i, K - 1, True)

                    @block.scalar
                    def _(act):
                        def keep_x(i):
                            for j in (0, 2):
                                wait_value(act, sem("x_psum"), 4 * i + (j + 1))
                                act.activation(xT[:, 2 * j:2 * j + 2, :].rearrange("p k t -> p (k t)"), fill_bank[j][:, 0:2 * WIDTH],
                                               ACT.Copy).then_inc(sem("xT_act"), 1)
                        n = n_items(act)
                        keep_x(0)
                        with act.Fori(0, n) as i:
                            for f in range(KF):
                                wait_value(act, sem("gc"), KF * i + (f + 1))
                                act.activation(sg[f % 2], gc[f % 2], ACT.Sigmoid, scale=SWIGLU_ALPHA).then_inc(sem("sg"), 1)
                            keep_x(i + 1)
                            for half in (0, 1):
                                wait_value(act, sem("y_psum"), K * i + 4 * (half + 1))
                                at = slice(half * BANK, (half + 1) * BANK)
                                act.activation(y_a[:, at], YA[:, :], ACT.Copy).then_inc(sem("y_kept"), 1)
                                act.activation(y_b[:, at], YB[0:REST, :], ACT.Copy).then_inc(sem("y_kept"), 1)
                            row = field(act, i, 4, 0, ROWS)
                            wait_value(act, sem("y_kept"), 4 * i + 4)
                            act.dma_start(y_dram[bass.ds(row, P), :], y_a).then_inc(sem("stored"), 16)
                            act.dma_start(y_dram[bass.ds(row + P, REST), :], y_b).then_inc(sem("stored"), 16)
                            wait_value(act, sem("stored"), 32 * i + 32)

                    @block.vector
                    def _(dve):
                        dve.memset(xg2[REST:TURN, :], 0.0).then_inc(sem("psum_set"), 1)
                        for bank in fill_bank:
                            dve.memset(bank[:, :], 0.0).then_inc(sem("psum_set"), 1)

                        def keep_x(i):
                            for j in (1, 3):
                                wait_value(dve, sem("x_psum"), 4 * i + (j + 1))
                                dve.tensor_copy(xT[:, 2 * j:2 * j + 2, :].rearrange("p k t -> p (k t)"), fill_bank[j][:, 0:2 * WIDTH]
                                                ).then_inc(sem("xT_dve"), 1)
                        n = n_items(dve)
                        keep_x(0)
                        for bank in (GU[0], GU[1], YB):
                            dve.memset(bank[:, :], 0.0).then_inc(sem("psum_set"), 1)
                        with dve.Fori(0, n) as i:
                            e = field(dve, i, 0, 0, E - 1)
                            dve.tensor_copy(bias[:, 0:KF], bias_gu[:, bass.ds(e * (2 * KF), KF)])
                            dve.tensor_scalar(bias[:, KF:2 * KF], bias_gu[:, bass.ds(e * (2 * KF) + KF, KF)], 1.0, None, ALU.add)
                            dve.tensor_copy(bias[:, 2 * KF:2 * KF + K], bias_dn[:, bass.ds(e * K, K)]).then_inc(sem("bias"), 1)
                            wait_value(dve, sem("bias"), i + 1)

                            def swiglu(f):
                                wait_value(dve, sem("sg"), KF * i + (f + 1))
                                dve.tensor_tensor(gs[f % 2], gc[f % 2], sg[f % 2], ALU.mult).then_inc(sem("gs"), 1)
                                wait_value(dve, sem("gs"), KF * i + (f + 1))
                                dve.scalar_tensor_tensor(actT[:, f, :], uc[f % 3], 1.0 - SWIGLU_LIMIT, gs[f % 2], ALU.max, ALU.mult).then_inc(sem("act"), 1)

                            for f in range(KF):
                                wait_value(dve, sem("gu_psum"), KF * i + (f + 1))
                                bank = GU[f % 3]
                                dve.tensor_scalar(gc[f % 2], bank[:, 0:WIDTH], bias[:, f:f + 1], SWIGLU_LIMIT, ALU.add, ALU.min).then_inc(sem("gc"), 1)
                                dve.tensor_scalar(uc[f % 3], bank[:, WIDTH:2 * WIDTH], bias[:, KF + f:KF + f + 1], 1.0 + SWIGLU_LIMIT,
                                                  ALU.add, ALU.min).then_inc(sem("gu_read"), 1)
                                if f:
                                    swiglu(f - 1)
                            swiglu(KF - 1)
                            keep_x(i + 1)
                            for d in range(K):
                                wait_value(dve, sem("dn_psum"), K * i + (d + 1))
                                if d >= 2:
                                    wait_value(dve, sem("y_psum"), K * i + (d - 1))
                                dve.tensor_scalar(yT[d % 2], DN[d % 2][:, 0:WIDTH], bias[:, 2 * KF + d:2 * KF + d + 1], None, ALU.add
                                                  ).then_inc(sem("yT"), 1)
                            wait_value(dve, sem("yT"), K * i + K)

        def combine():
            ctx, sem = stage("comb")
            with ctx:
                w_gate = view(arena_h, 0, K, D)
                w_emb = view(arena_m, 4096, KP, D)
                yg = [[view(arena_w, D * (4 * b + j), D) for j in range(TOP_K)] for b in (0, 1)]
                x1, x2, xn, outt = ([view(arena_w, D * (8 + 2 * j + b), D) for b in (0, 1)] for j in range(4))
                xnT = [view(arena_w, D * (16 + b), K, P) for b in (0, 1)]
                pt = [view(arena_m, 6144 + PLE * b, PLE) for b in (0, 1)]
                pT = [view(arena_m, 6144 + PLE * (2 + b), KP, P) for b in (0, 1)]
                sig, junk = view(arena_w, D * 20, D), view(arena_m, 0, D)
                dst = [view(arena_w, D * 21 + 4 * b, TOP_K).bitcast(I32) for b in (0, 1)]
                gts = [view(arena_w, D * 21 + 8 + 4 * b, TOP_K) for b in (0, 1)]
                ms, rms, rstd = (view(arena_w, D * 21 + 16 + j, 1) for j in range(3))
                TB0, TB1, TP = banks[0:3]
                gate_bank, emb_bank = banks[4:6], banks[6:8]
                with nc.Block() as block:
                    @block.sync
                    def _(sp):
                        for b in (0, 1):
                            if b:
                                sp.wait_ge(sem("y0"), 64)
                            sp.dma_start(x1[b], x1_dram[b * P:(b + 1) * P, :]).then_inc(sem(f"x{b}"), 16)
                            sp.dma_start(pt[b], p2d[b * P:(b + 1) * P, :]).then_inc(sem(f"x{b}"), 16)

                        def store(n, b):
                            wait_value(sp, sem("out"), n + 1)
                            sp.dma_start(out2d[bass.ds(n * P, P), :], outt[b]).then_inc(sem("stored"), 16)
                            wait_value(sp, sem("stored"), 16 * n + 16)
                            sp.sem_inc(sem("rows_free"), 1)

                        sp.sem_inc(sem("rows_free"), 2)
                        with sp.Fori(0, T // 2 - 1) as i:
                            for b in (0, 1):
                                wait_value(sp, sem("summed"), 2 * i + (b + 1))
                                wait_value(sp, sem("xnT_psum"), 2 * i + (b + 1))
                                rows = bass.ds(i * (2 * P) + (2 + b) * P, P)
                                sp.dma_start(x1[b], x1_dram[rows, :]).then_inc(sem(f"x{b}"), 16)
                                sp.dma_start(pt[b], p2d[rows, :]).then_inc(sem(f"x{b}"), 16)
                                store(2 * i + b, b)
                        store(T - 2, 0)
                        store(T - 1, 1)

                    @block.gpsimd
                    def _(pool):
                        def gather(n, b):
                            if not isinstance(n, int):
                                wait_value(pool, sem("summed"), n - 1)
                            pool.tensor_copy(gts[b], gates_all[:, bass.ds(n, 1), :].rearrange("p o k -> p (o k)")).then_inc(sem("dst"), 1)
                            pool.tensor_copy(dst[b], dest_all[:, bass.ds(n, 1), :].rearrange("p o k -> p (o k)")).then_inc(sem("dst"), 1)
                            wait_value(pool, sem("dst"), 2 * n + 2)
                            for j in range(TOP_K):
                                pool.indirect_dma_start(yg[b][j], None, y_dram[0:ROWS, :], bass.IndirectOffsetOnAxis(dst[b][:, j:j + 1], 0)
                                                        ).then_inc(sem(f"y{b}"), 16)
                        gather(0, 0)
                        gather(1, 1)
                        pair_loop(pool, T, gather, first=2)

                    @block.vector
                    def _(dve):
                        def norm(n, b):
                            wait_value(dve, sem(f"x{b}"), 16 * n + (32 - 16 * b))
                            wait_value(dve, sem(f"y{b}"), 32 * n + (64 - 32 * b))
                            for j in range(TOP_K):
                                last = j == TOP_K - 1
                                dve.scalar_tensor_tensor(x2[b], yg[b][j], gts[b][:, j:j + 1], x1[b] if j == 0 else x2[b],
                                                         ALU.mult, ALU.add).then_inc(sem("summed" if last else "part"), 1)
                                if last:
                                    wait_value(dve, sem("summed"), n + 1)
                                else:
                                    wait_value(dve, sem("part"), 3 * n + (j + 1))
                            wait_value(dve, sem("rms"), n + 1)
                            dve.reciprocal(rstd, rms).then_inc(sem("rstd"), 1)
                            wait_value(dve, sem("rstd"), n + 1)
                            dve.scalar_tensor_tensor(xn[b], x2[b], rstd, gain_row[:, :], ALU.mult, ALU.mult).then_inc(sem("xn"), 1)

                        def keep(n, b):
                            wait_value(dve, sem("xnT_psum"), n + 1)
                            dve.tensor_copy(xnT[b][:, 4:8, :].rearrange("p k t -> p (k t)"), TB1[:, :]).then_inc(sem("xnT"), 1)

                        def finish(n, b):
                            wait_value(dve, sem("sig"), 2 * n + 2)
                            wait_value(dve, sem("emb_psum"), n + 1)
                            wait_value(dve, sem("rows_free"), n + 1)
                            for j in (0, 1):
                                half = slice(j * BANK, (j + 1) * BANK)
                                dve.tensor_tensor(outt[b][:, half], emb_bank[j][:, :], sig[:, half], ALU.mult).then_inc(sem("gated"), 1)
                            wait_value(dve, sem("gated"), 2 * n + 2)
                            dve.tensor_tensor(outt[b], outt[b], x2[b], ALU.add).then_inc(sem("out"), 1)
                            wait_value(dve, sem("out"), n + 1)

                        def ready(n, b):
                            norm(n, b)
                            keep(n, b)
                        ahead_loop(dve, T, ready, nothing, finish)

                    @block.scalar
                    def _(act):
                        def norm(n, b):
                            wait_value(act, sem("summed"), n + 1)
                            act.activation(junk, x2[b], ACT.Square, scale=float(D) ** -0.5, accum_out=ms).then_inc(sem("ms"), 1)
                            wait_value(act, sem("ms"), n + 1)
                            act.activation(rms, ms, ACT.Sqrt, bias=eps[:, :]).then_inc(sem("rms"), 1)

                        def keep(n, b):
                            wait_value(act, sem("xnT_psum"), n + 1)
                            act.activation(xnT[b][:, 0:4, :].rearrange("p k t -> p (k t)"), TB0[:, :], ACT.Copy).then_inc(sem("xnT"), 1)
                            act.activation(pT[b].rearrange("p k t -> p (k t)"), TP[:, 0:KP * P], ACT.Copy).then_inc(sem("xnT"), 1)

                        def gate(n, b):
                            wait_value(act, sem("gate_psum"), n + 1)
                            if isinstance(n, int) and n == T - 1:
                                act.wait_ge(sem("out"), T - 1)
                            for j in (0, 1):
                                act.activation(sig[:, j * BANK:(j + 1) * BANK], gate_bank[j][:, :], ACT.Sigmoid).then_inc(sem("sig"), 1)

                        def ready(n, b):
                            norm(n, b)
                            keep(n, b)
                        ahead_loop(act, T, ready, nothing, gate)

                    @block.tensor
                    def _(pe):
                        def turn(n, b):
                            wait_value(pe, sem("xn"), n + 1)
                            wait_value(pe, sem(f"x{b}"), 16 * n + (32 - 16 * b))
                            for k in range(K):
                                pe.transpose((TB0, TB1)[k // 4][:, (k % 4) * P:(k % 4 + 1) * P], xn[b][:, k * P:(k + 1) * P], ident[:, :])
                            for k in range(KP):
                                m = pe.transpose(TP[:, k * P:(k + 1) * P], pt[b][:, k * P:(k + 1) * P], ident[:, :])
                            m.then_inc(sem("xnT_psum"), 1)

                        def gate(n, b):
                            wait_value(pe, sem("xnT"), 3 * n + 3)
                            if not (isinstance(n, int) and n == 0):
                                wait_value(pe, sem("sig"), 2 * n)
                            for j in (0, 1):
                                for k in range(K):
                                    m = pe.matmul(gate_bank[j][:, :], xnT[b][:, k, :], w_gate[:, k, j * BANK:(j + 1) * BANK],
                                                  start=(k == 0), stop=(k == K - 1))
                            m.then_inc(sem("gate_psum"), 1)

                        def embed(n, b):
                            if isinstance(n, int) and n == T - 1:
                                pe.wait_ge(sem("out"), T - 1)
                            for j in (0, 1):
                                for k in range(KP):
                                    m = pe.matmul(emb_bank[j][:, :], pT[b][:, k, :], w_emb[:, k, j * BANK:(j + 1) * BANK],
                                                  start=(k == 0), stop=(k == KP - 1))
                            m.then_inc(sem("emb_psum"), 1)
                        ahead_loop(pe, T, turn, gate, embed)

        front()
        pool_branch()
        attend()
        merge()
        route()
        experts()
        combine()


INS = ["x", "p", "positions", "g_mix", "w_in", "g_q_lat", "w_q_b", "g_kv_lat", "w_kv_b", "g_q_head",
       "g_k_nope", "g_k_rope", "w_pool", "pool_scale", "w_attn_out", "w_pool_out", "w_o", "g_ffn",
       "w_router", "b_router", "w_gate_up", "b_gate_up", "w_down", "b_down", "g_ple", "w_ple_gate", "w_ple"]


def kernel(**inputs):
    import concourse.bacc as bacc
    from concourse.bass_utils import run_bass_kernel_spmd

    nc = bacc.Bacc("TRN2", target_bir_lowering=False, num_devices=1)
    arrays, args = {}, []
    for name in INS:
        a = np.ascontiguousarray(inputs[name])
        arrays[f"in_{name}_dram"] = a
        args.append(nc.dram_tensor(f"in_{name}_dram", a.shape, mybir.dt.from_np(a.dtype), kind="ExternalInput").ap())
    shape = inputs["x"].shape
    args.append(nc.dram_tensor("out_0_dram", shape, F32, kind="ExternalOutput").ap())
    build(nc, *args)
    r = run_bass_kernel_spmd(nc, [arrays], core_ids=[0])
    return r.results[0]["out_0_dram"]
```
